# Optimizing a Trainium2 kernel written in Bass

```python
import jax, jax.numpy as jnp
from jax import lax
import numpy as np

D_MODEL = 1024
BATCH = 1
SEQ = 1024
DEPTH = 1

SB_HEADS = 8
SB_HEAD_DIM = 64
SB_WIDTH = SB_HEADS * SB_HEAD_DIM
Q_BLOCK = 128
ML_HEADS = 4
ML_HEAD_DIM = 128
ML_WIDTH = ML_HEADS * ML_HEAD_DIM
ML_CHUNK = 64
CONV_WIDTH = 4
N_BRANCH = 2
SPLIT_SIZES = (SB_WIDTH, SB_WIDTH, SB_WIDTH, SB_WIDTH,
               ML_WIDTH, ML_WIDTH, ML_WIDTH, ML_WIDTH, ML_WIDTH,
               ML_HEADS, ML_HEADS, D_MODEL, D_MODEL)
IN_COLS = 4 * SB_WIDTH + 5 * ML_WIDTH + 2 * ML_HEADS + N_BRANCH * D_MODEL
F_GATE_OFFSET = 4 * SB_WIDTH + 5 * ML_WIDTH + ML_HEADS
DEEPNORM_ALPHA = (2.0 * DEPTH) ** 0.25
DEEPNORM_BETA = (8.0 * DEPTH) ** -0.25
LN_EPS = 1e-5

kernel_name = "hybrid_stickbreak_mlstm_deepnorm_adaln"

def layer_norm(x, g, b):
    xf = x.astype(jnp.float32)
    mu = xf.mean(-1, keepdims=True)
    var = jnp.mean(jnp.square(xf - mu), -1, keepdims=True)
    return ((xf - mu) * lax.rsqrt(var + LN_EPS) * g + b).astype(x.dtype)

def causal_depthwise_conv(x, w, b):
    C = x.shape[-1]
    y = lax.conv_general_dilated(
        x, w[:, None, :].astype(x.dtype), window_strides=(1,),
        padding=[(CONV_WIDTH - 1, 0)], dimension_numbers=('NWC', 'WIO', 'NWC'),
        feature_group_count=C)
    return y + b

def to_heads(a, n_heads):
    B, S, W = a.shape
    return a.reshape(B, S, n_heads, W // n_heads).transpose(0, 2, 1, 3)

def from_heads(a):
    B, H, S, d = a.shape
    return a.transpose(0, 2, 1, 3).reshape(B, S, H * d)

def stick_breaking_attention(q, k, v):
    B, H, S, d = q.shape
    scale = d ** -0.5
    outs = []
    for blk in range(S // Q_BLOCK):
        q0 = blk * Q_BLOCK
        kend = q0 + Q_BLOCK
        qb = q[:, :, q0:kend]
        kb = k[:, :, :kend]
        vb = v[:, :, :kend]
        z = jnp.einsum('bhtd,bhsd->bhts', qb, kb).astype(jnp.float32) * scale
        t_idx = q0 + jnp.arange(Q_BLOCK)[:, None]
        s_idx = jnp.arange(kend)[None, :]
        causal = s_idx < t_idx
        log_beta = jax.nn.log_sigmoid(z)
        log_rem = jnp.where(causal, jax.nn.log_sigmoid(-z), 0.0)
        suffix = lax.cumsum(log_rem, axis=3, reverse=True) - log_rem
        attn = jnp.where(causal, jnp.exp(log_beta + suffix), 0.0)
        outs.append(jnp.einsum('bhts,bhsd->bhtd', attn.astype(vb.dtype), vb))
    return jnp.concatenate(outs, axis=2)

def mlstm_chunkwise(q, k, v, i_pre, log_f):
    B, H, S, dk = q.shape
    dv = v.shape[-1]
    L = ML_CHUNK
    NC = S // L
    q = q.astype(jnp.float32) * dk ** -0.5
    k = k.astype(jnp.float32)
    v = v.astype(jnp.float32)

    def to_chunks(a):
        return jnp.moveaxis(a.reshape(B, H, NC, L, *a.shape[3:]), 2, 0)

    xs = (to_chunks(q), to_chunks(k), to_chunks(v), to_chunks(i_pre), to_chunks(log_f))
    causal = jnp.tril(jnp.ones((L, L), dtype=bool))

    def step(carry, xs_c):
        C, n, m = carry
        qb, kb, vb, ib, fb = xs_c
        b = jnp.cumsum(fb, axis=-1)
        b_last = b[..., -1]
        D = jnp.where(causal, b[..., :, None] - b[..., None, :] + ib[..., None, :], -jnp.inf)
        inter = b + m[..., None]
        m_t = jnp.maximum(inter, D.max(-1))
        w_inter = jnp.exp(inter - m_t)
        s_mat = jnp.exp(D - m_t[..., None]) * jnp.einsum('bhtd,bhsd->bhts', qb, kb)
        num = (w_inter[..., None] * jnp.einsum('bhtd,bhde->bhte', qb, C)
               + jnp.einsum('bhts,bhse->bhte', s_mat, vb))
        den = w_inter * jnp.einsum('bhtd,bhd->bht', qb, n) + s_mat.sum(-1)
        h = num / jnp.maximum(jnp.abs(den), jnp.exp(-m_t))[..., None]
        g = b_last[..., None] - b + ib
        m_new = jnp.maximum(b_last + m, g.max(-1))
        decay = jnp.exp(b_last + m - m_new)
        wk = jnp.exp(g - m_new[..., None])
        C_new = decay[..., None, None] * C + jnp.einsum('bhs,bhsd,bhse->bhde', wk, kb, vb)
        n_new = decay[..., None] * n + jnp.einsum('bhs,bhsd->bhd', wk, kb)
        return (C_new, n_new, m_new), h

    init = (jnp.zeros((B, H, dk, dv), jnp.float32),
            jnp.zeros((B, H, dk), jnp.float32),
            jnp.zeros((B, H), jnp.float32))
    _, hs = lax.scan(step, init, xs)
    return jnp.moveaxis(hs, 0, 2).reshape(B, H, S, dv)

def head_norm(h, g):
    mu = h.mean(-1, keepdims=True)
    var = jnp.mean(jnp.square(h - mu), -1, keepdims=True)
    return from_heads((h - mu) * lax.rsqrt(var + LN_EPS)) * g

def hybrid_layer(x, c, w_ada, b_ada, w_in, b_in, conv_w, conv_b, ml_norm_g,
                 w_sb_proj, w_ml_proj, w_out, ln_g, ln_b):
    dtype = x.dtype
    mod = jax.nn.silu(c) @ w_ada + b_ada
    shift, scale, gate = jnp.split(mod, 3, axis=-1)
    h = x * (1.0 + scale[:, None, :]) + shift[:, None, :]

    proj = h @ w_in + b_in
    points = []
    acc = 0
    for size in SPLIT_SIZES[:-1]:
        acc += size
        points.append(acc)
    (sb_q, sb_k, sb_v, sb_z, ml_q, ml_k, ml_v, ml_o, ml_z,
     ml_i, ml_f, g_sb, g_ml) = jnp.split(proj, points, axis=-1)

    y_sb = stick_breaking_attention(to_heads(sb_q, SB_HEADS), to_heads(sb_k, SB_HEADS),
                                    to_heads(sb_v, SB_HEADS))
    y_sb = (from_heads(y_sb) * jax.nn.silu(sb_z)) @ w_sb_proj

    qk = jax.nn.silu(causal_depthwise_conv(jnp.concatenate([ml_q, ml_k], -1), conv_w, conv_b))
    mq, mk = jnp.split(qk, 2, axis=-1)
    i_pre = ml_i.astype(jnp.float32).transpose(0, 2, 1)
    log_f = jax.nn.log_sigmoid(ml_f.astype(jnp.float32)).transpose(0, 2, 1)
    hm = mlstm_chunkwise(to_heads(mq, ML_HEADS), to_heads(mk, ML_HEADS),
                         to_heads(ml_v, ML_HEADS), i_pre, log_f)
    hm = head_norm(hm, ml_norm_g).astype(dtype)
    y_ml = (hm * jax.nn.sigmoid(ml_o) * jax.nn.silu(ml_z)) @ w_ml_proj

    y = (jax.nn.sigmoid(g_sb) * y_sb + jax.nn.sigmoid(g_ml) * y_ml) @ w_out

    return layer_norm(DEEPNORM_ALPHA * x + (1.0 + gate[:, None, :]) * y, ln_g, ln_b)

def setup_inputs(seed: int = 0) -> dict:
    key = jax.random.key(seed)
    ks = jax.random.split(key, 14)
    D = D_MODEL
    nrm = lambda k, shape: jax.random.normal(k, shape, jnp.float32)
    x = nrm(ks[0], (BATCH, SEQ, D))
    c = nrm(ks[1], (BATCH, D))
    w_ada = nrm(ks[2], (DEPTH, D, 3 * D)) * (0.1 * D ** -0.5)
    b_ada = 0.01 * nrm(ks[3], (DEPTH, 3 * D))
    w_in = nrm(ks[4], (DEPTH, D, IN_COLS)) * D ** -0.5
    b_in = 0.02 * nrm(ks[5], (DEPTH, IN_COLS))
    b_in = b_in.at[:, F_GATE_OFFSET:F_GATE_OFFSET + ML_HEADS].add(
        jnp.linspace(3.0, 6.0, ML_HEADS, dtype=jnp.float32))
    conv_w = nrm(ks[6], (DEPTH, CONV_WIDTH, 2 * ML_WIDTH)) * CONV_WIDTH ** -0.5
    conv_b = 0.02 * nrm(ks[7], (DEPTH, 2 * ML_WIDTH))
    ml_norm_g = 1.0 + 0.02 * nrm(ks[8], (DEPTH, ML_WIDTH))
    w_sb_proj = nrm(ks[9], (DEPTH, SB_WIDTH, D)) * (SB_WIDTH ** -0.5 * DEEPNORM_BETA)
    w_ml_proj = nrm(ks[10], (DEPTH, ML_WIDTH, D)) * (ML_WIDTH ** -0.5 * DEEPNORM_BETA)
    w_out = nrm(ks[11], (DEPTH, D, D)) * (D ** -0.5 * DEEPNORM_BETA)
    ln_g = 1.0 + 0.02 * nrm(ks[12], (DEPTH, D))
    ln_b = 0.02 * nrm(ks[13], (DEPTH, D))
    return {"x": x, "c": c, "w_ada": w_ada, "b_ada": b_ada, "w_in": w_in, "b_in": b_in,
            "conv_w": conv_w, "conv_b": conv_b, "ml_norm_g": ml_norm_g,
            "w_sb_proj": w_sb_proj, "w_ml_proj": w_ml_proj, "w_out": w_out,
            "ln_g": ln_g, "ln_b": ln_b}

def reference(x, c, w_ada, b_ada, w_in, b_in, conv_w, conv_b, ml_norm_g,
              w_sb_proj, w_ml_proj, w_out, ln_g, ln_b):
    for l in range(DEPTH):
        x = hybrid_layer(x, c, w_ada[l], b_ada[l], w_in[l], b_in[l], conv_w[l], conv_b[l],
                         ml_norm_g[l], w_sb_proj[l], w_ml_proj[l], w_out[l], ln_g[l], ln_b[l])
    return x


_drawn_inputs = setup_inputs


def setup_inputs(seed=0):
    import zlib

    import numpy as np

    out = dict(_drawn_inputs(seed))
    spreads = {}
    factors = {'b_ada': 8.0, 'conv_b': 8.0, 'ml_norm_g': 8.0, 'ln_g': 2.89, 'ln_b': 2.747}
    for name, (base, spread) in spreads.items():
        noise = np.random.default_rng([zlib.crc32(name.encode()), seed]).standard_normal(out[name].shape)
        drawn = base * np.exp(spread * noise) if base else spread * noise
        out[name] = __import__('jax').numpy.asarray(drawn.astype(out[name].dtype))
    for name, factor in factors.items():
        out[name] = (out[name] * factor).astype(out[name].dtype)
    return out
```

```python
from contextlib import ExitStack

import concourse.bass as bass
from concourse import mybir

ALU = mybir.AluOpType
ACT = mybir.ActivationFunctionType
F32 = mybir.dt.float32
F32R = mybir.dt.float32r

P = 128
D = 1024
S = 1024
KT = D // P
HALF = 512
W_SB = 512
W_ML = 512
NH = W_ML // P
NC = S // P
SB_SCALE = 64 ** -0.5
ML_SCALE = 128 ** -0.5
ALPHA = 2.0 ** 0.25
EPS = 1e-5
SOFT_CAP = 30.0
EXP_CAP = 2.0 ** 62

OFF_SB = [0, W_SB, 2 * W_SB, 3 * W_SB]
OFF_ML = [4 * W_SB + n * W_ML for n in range(5)]
OFF_IF = 4 * W_SB + 5 * W_ML
OFF_GSB = OFF_IF + 2 * NH
OFF_GML = OFF_GSB + D

ROW_B = 0
ROW_GSB = 36
ROW_GML = 44
ROW_CW = 52
ROW_CB = 84
ROW_NG = 92
ROW_ADA = 96
ROW_C = 120

JOB_MM = 3 * KT * 2
PRO_JOBS = 5
JOBS = ["mlk", "mlq", "mlv", "mlo", "mlz", "sbq", "sbk", "sbv", "sbz"]
JOBS_LAST = JOBS[:5] + ["gsb", "gml"]
NJ = len(JOBS)
END_JOBS = PRO_JOBS + (NH - 1) * NJ + len(JOBS_LAST) - 2
END_CHUNKS = 2 * END_JOBS

SLOTS = [(tc, j) for tc in range(2) for j in range(4 * tc + 3, -1, -1)]
NS = len(SLOTS)


def first_col(s):
    tc, j = SLOTS[s]
    return max(0, P * (j - 4 * tc))


def diagonal(s):
    tc, j = SLOTS[s]
    return j >= 4 * tc


def opens(s):
    tc, j = SLOTS[s]
    return j == 4 * tc + 3


def closes(s):
    return SLOTS[s][1] == 0


def diagonals(s):
    return sum(diagonal(x) for x in range(s))


def carries(s):
    return sum(not closes(x) for x in range(s))


ND, NCAR = diagonals(NS), carries(NS)
PRE = 48


def segments(last):
    at, out = PRE, []
    for s in range(NS):
        sizes = (10, 10, 12) if s < 3 else (6, 7, 7) if last else (10, 10, 11)
        row = [at]
        for n in sizes:
            at += n
            row.append(at)
        out.append(row)
    return out, JOB_MM * (len(JOBS_LAST) if last else NJ)


def events(lo, hi, last):
    n = len(JOBS_LAST) if last else NJ
    found = [(JOB_MM * 4 + 6, 2, "o_log", 0, 0), (JOB_MM * 5 + 6, 2, "z_log", 0, 0),
             (JOB_MM * 5 + 14, 2, "z_exp", 0, 0), (JOB_MM * 5 + 22, 2, "z_mul", 0, 0)]
    for j in range(n):
        found += [(JOB_MM * j + 24, 0, "evac", j, 0), (JOB_MM * (j + 1), 0, "evac", j, 1)]
    for c in range(2, 2 * n + 2):
        j, odd = divmod(c - 3, 2)
        found.append((JOB_MM * j + 36 + 12 * odd, 1, "split", c, 0))
    return [e[2:] for e in sorted(found) if lo < e[0] <= hi]


class Chain:

    def __init__(self, eng, semaphore):
        self.eng, self.semaphore, self.base, self.k, self.i, self.per = eng, semaphore, 0, 0, 0, 0

    def enter(self, i, per):
        self.i, self.per, self.k = i, per, 0

    def leave(self, rounds, where):
        assert self.k == self.per, (where, self.k, self.per)
        self.base, self.k, self.i, self.per = self.base + rounds * self.per, 0, 0, 0

    def mark(self, instruction):
        self.k += 1
        instruction.then_inc(self.semaphore, 1)

    def wait(self):
        self.eng.wait_ge(self.semaphore, self.i * self.per + (self.base + self.k))

    def __call__(self, instruction):
        self.mark(instruction)
        self.wait()


def build_kernel(nc, x, c, w_ada, b_ada, w_in, b_in, conv_w, conv_b, ml_norm_g, w_sb_proj, w_ml_proj, w_out,
                 ln_g, ln_b, out):
    ysb_dram = nc.dram_tensor("ysb_scratch", (NH, P, S), F32, kind="Internal").ap()
    yml_dram = nc.dram_tensor("yml_scratch", (NH, P, S), F32, kind="Internal").ap()
    w_in_v = w_in[0].rearrange("(k p) c -> p k c", p=P)
    w_ada_v = w_ada[0].rearrange("(k p) c -> p k c", p=P)
    w_sbp_v = w_sb_proj[0].rearrange("(k p) c -> p k c", p=P)
    w_mlp_v = w_ml_proj[0].rearrange("(k p) c -> p k c", p=P)
    w_out_v = w_out[0].rearrange("(k p) c -> p k c", p=P)
    x_v = x[0].rearrange("(t p) d -> p t d", p=P)
    out_v = out[0].rearrange("(t p) d -> p t d", p=P)

    with ExitStack() as ctx:
        def sb(name, shape, dt=F32, to=None):
            return (to or ctx).enter_context(nc.sbuf_tensor(name, shape, dt))

        def sem(name):
            return ctx.enter_context(nc.semaphore(name))

        bank = [ctx.enter_context(nc.psum_tensor(f"bank{n}", [P, HALF], F32)) for n in range(8)]
        proj_ps, z_ps, y_ps, misc_ps = bank[0:2], bank[2:4], bank[4], bank[5:8]

        hH = sb("hH", [P, KT, S], F32R)
        hL = sb("hL", [P, KT, S], F32R)
        w_raw = sb("w_raw", [P, 3, 4, P])
        wH = sb("wH", [P, 3, 4, P], F32R)
        wL = sb("wL", [P, 3, 4, P], F32R)
        cols = sb("cols", [P, P])
        ncols = sb("ncols", [P, P])
        silu_c = sb("silu_c", [P, KT])
        r_bias = sb("r_bias", [P, 1])
        ident = sb("ident", [P, P])
        ones = sb("ones", [P, P])
        stat_out = sb("stat_out", [P, 2, 2, 6])
        small = sb("small", [P, 48])

        loop = ExitStack()
        lt = lambda name, shape, dt=F32: sb(name, shape, dt, loop)
        next_q, next_k = lt("next_q", [P, S]), lt("next_k", [P, S])
        later = lt("later", [P, P])
        notbefore = lt("notbefore", [P, P])
        neg_upto = lt("neg_upto", [P, P], F32R)
        neg_ones = lt("neg_ones", [P, P], F32R)
        next_v, next_g = lt("next_v", [P, S]), lt("next_g", [P, S])
        sel_all = lt("sel_all", [P, NH, P])
        tok = lt("tok", [P, NC, 4, NH])
        dec = lt("dec", [P, NC, NH])
        bm = lt("bm", [P, S])
        sig = lt("sig", [P, S])
        inner = ExitStack()
        it = lambda name, shape, dt=F32: sb(name, shape, dt, inner)
        qH, qL = it("qH", [P, S], F32R), it("qL", [P, S], F32R)
        kH, kL = it("kH", [P, S], F32R), it("kL", [P, S], F32R)
        v_tok = it("v_tok", [P, NC, P])
        g_cur = it("g_cur", [P, S])
        soft = [it(f"soft{h}", [P, HALF]) for h in range(2)]
        spH = [it(f"spH{h}", [P, HALF], F32R) for h in range(2)]
        spL = [it(f"spL{h}", [P, HALF], F32R) for h in range(2)]
        tsum = [it(f"tsum{h}", [P, HALF]) for h in range(2)]
        tsH = [it(f"tsH{h}", [P, HALF], F32R) for h in range(2)]
        tsL = [it(f"tsL{h}", [P, HALF], F32R) for h in range(2)]
        y_stage = it("y_stage", [P, HALF])
        conv_in = it("conv_in", [P, 4 + S])
        m_q, m_k = it("m_q", [P, S]), it("m_k", [P, S])
        m_vraw = it("m_vraw", [P, S])
        m_gate = it("m_gate", [P, S])
        m_ktok = it("m_ktok", [P, NC, P])
        m_vtok = it("m_vtok", [P, NC, P + 1])
        m_num = it("m_num", [P, NC, P + 1])
        m_w = it("m_w", [P, NC, P])
        m_state = it("m_state", [P, P + 1])
        m_s = it("m_s", [P, P])
        m_tmp = it("m_tmp", [P, P + 1])
        h_tok = it("h_tok", [P, 4, NC])
        h_dec = it("h_dec", [P, NC])
        h_col = it("h_col", [P, 56])
        sel_cur = it("sel_cur", [P, P])
        stat = it("stat", [P, NC, 6])
        mv = it("mv", [P, NC, 2])
        inner.close()
        pro = ExitStack()
        pt = lambda name, shape, dt=F32: sb(name, shape, dt, pro)
        x_rows = pt("x_rows", [P, NC, D])
        a_raw = pt("a_raw", [P, 3, KT, P])
        upto = pt("upto", [P, P])
        prm = pt("prm", [P, P])
        mod = pt("mod", [P, 2, KT])
        xT = pt("xT", [P, KT, S])
        pro.close()
        rows_ctx = ExitStack()
        rt = lambda name, shape, dt=F32: sb(name, shape, dt, rows_ctx)
        r_i, r_f, r_e = rt("r_i", [P, S]), rt("r_f", [P, S]), rt("r_e", [P, S])
        r_b, r_m, r_q = rt("r_b", [P, S]), rt("r_m", [P, S]), rt("r_q", [P, S])
        r_one = rt("r_one", [P, S])
        r_if = rt("r_if", [P, S])
        rows_ctx.close()
        loop.close()
        after = ExitStack()
        at = lambda name, shape, dt=F32: sb(name, shape, dt, after)
        sigs, sigm = at("sigs", [P, S]), at("sigm", [P, S])
        yT = at("yT", [P, KT, S])
        m_prod = at("m_prod", [P, HALF])
        raw = at("raw", [P, D])
        g_acc = at("g_acc", [P, D])
        merge = ExitStack()
        mt = lambda name, shape, dt=F32: sb(name, shape, dt, merge)
        ybH = [mt("ysbH", [P, NH, S], F32R), mt("ymlH", [P, NH, S], F32R)]
        ybL = [mt("ysbL", [P, NH, S], F32R), mt("ymlL", [P, NH, S], F32R)]
        merge.close()
        yH = at("yH", [P, 2, KT, P], F32R)
        yL = at("yL", [P, 2, KT, P], F32R)
        x_in = at("x_in", [P, 2, D])
        res = at("res", [P, 2, D])
        gate1, lng, lnb = at("gate1", [P, D]), at("lng", [P, D]), at("lnb", [P, D])
        after.close()

        params_in, x_rows_in, bias_in = sem("params_in"), sem("x_rows_in"), sem("bias_in")
        a_in = [sem(f"ada_in{n}") for n in range(3)]
        w_in_s = [sem(f"weights_in{n}") for n in range(3)]
        consts, consts_r = sem("consts_made"), sem("consts_rounded")
        cols_done, c_exp, silu_done = sem("cols_done"), sem("c_exp"), sem("silu_done")
        ada_used, ada_done, mod_done = sem("ada_used"), sem("ada_done"), sem("mod_done")
        h_full, hH_done, hL_done = sem("h_full"), sem("hH_done"), sem("hL_done")
        rows_zero, rows_in, f_ln = sem("rows_zero"), sem("rows_in"), sem("f_ln")
        q_rows, q_exp, tok_done = sem("q_rows"), sem("q_exp"), sem("tok_done")
        wH_done, wL_done = sem("wH_done"), sem("wL_done")
        w_first_used = sem("w_first_used")
        filled = [sem(f"proj_filled{h}") for h in range(2)]
        drained = [sem(f"proj_drained{h}") for h in range(2)]
        m_filled = [sem(f"misc_filled{n}") for n in range(3)]
        m_drained = [sem(f"misc_drained{n}") for n in range(3)]
        sig_exp, sig_capped, sig_log, sig_done = sem("sig_exp"), sem("sig_capped"), sem("sig_log"), sem("sig_done")
        sig_used, g_made = sem("sig_used"), sem("g_made")
        o_capped, o_log, z_sum, m_gate_done = sem("o_capped"), sem("o_log"), sem("z_sum"), sem("m_gate_done")
        two = lambda name: [sem(f"{name}{h}") for h in range(2)]
        z_done, ex_done, ln_done = two("z_done"), two("ex_done"), two("ln_done")
        sp_raw, sp_done, spH_done, spL_done = two("sp_raw"), two("sp_done"), two("spH_done"), two("spL_done")
        ts_zero, ts_sum, tsH_done, tsL_done = two("ts_zero"), two("ts_sum"), two("tsH_done"), two("tsL_done")
        e_done, a_exp, a_mask, pv_done = two("e_done"), two("a_exp"), two("a_mask"), two("pv_done")
        y_staged, y_stored = sem("y_staged"), sem("y_stored")
        pair_split, h_cols = sem("pair_split"), sem("h_cols_done")
        conv_acc, conv_done, conv_pad = sem("conv_acc"), sem("conv_done"), sem("conv_pad")
        conv_exp, conv_cap, conv_log, conv_sig = sem("conv_exp"), sem("conv_cap"), sem("conv_log"), sem("conv_sig")
        w_sum, w_exp, w_mask = sem("w_sum"), sem("w_exp"), sem("w_mask")
        state_zero, qc_done = sem("state_zero"), sem("qc_done")
        var_done, rstd_ln, rstd_exp = sem("var_done"), sem("rstd_ln"), sem("rstd_exp")
        hn_done, yml_stored = sem("hn_done"), sem("yml_stored")
        dve_step = sem("dve_step")
        y_in, yb_H, yb_L = [sem("ysb_in"), sem("yml_in")], sem("yb_H"), sem("yb_L")
        raw_in, g_acc_step = sem("raw_in"), sem("g_acc_step")
        wo_in = [sem("w_out_in0"), sem("w_out_in1")]
        woH_done, woL_done = sem("woH_done"), sem("woL_done")
        two_ = lambda name: [sem(f"{name}_sb"), sem(f"{name}_ml")]
        g_capped, g_log, g_done = two_("gate_capped"), two_("gate_log"), two_("gate_sigmoid")
        yT_done, yH_done, yL_done, bc_in = sem("yT_done"), sem("yH_done"), sem("yL_done"), sem("broadcast_in")
        x_tile_in = [sem("x_tile_in0"), sem("x_tile_in1")]
        stored = [sem("stored0"), sem("stored1")]
        out_done, gate_done = sem("out_done"), sem("gate_done")

        block = ctx.enter_context(nc.Block())

        M_PRO, M_PER = [10, 9, 1], [13, 13, 8]
        F_V, F_R, F_MK, F_MV, F_CHUNK, F_HN = 0, 1, 2, 3, 4, 12

        def m_count(n, i, k):
            return i * M_PER[n] + (M_PRO[n] + k)

        def job(i, j):
            return i * NJ + (PRO_JOBS + j)

        def chunk(i, c_):
            return i * 2 * NJ + (2 * PRO_JOBS + c_)

        def halves(h):
            return slice(h * HALF, (h + 1) * HALF)

        GROUP = {"sbq": 0, "sbk": 1, "sbv": 2, "sbz": 3, "mlq": 4, "mlk": 5, "mlv": 6, "mlo": 7, "mlz": 8}
        H_NEXT, H_TAP, H_CB, H_NG, H_NEG = 9, {"q": 18, "k": 22}, {"q": 26, "k": 27}, 28, 32

        def bias_of(name, negative=False):
            n = GROUP[name] + (H_NEXT if name[:2] == "sb" else 0) + (H_NEG if negative else 0)
            return h_col[:, n:n + 1]

        @block.sync
        def _(sp):
            bi = b_in[0]
            rows = [
                (ROW_C, c[0]), (ROW_ADA, b_ada[0]), (ROW_B, bi[0:OFF_IF]),
                (ROW_GSB, bi[OFF_GSB:OFF_GSB + 2 * D]), (ROW_CB, conv_b[0]), (ROW_NG, ml_norm_g[0]),
            ]
            for row, src in rows:
                src = src.rearrange("(t p) -> t p", p=P)
                sp.dma_start(prm[row:row + src.shape[0], :], src).then_inc(params_in, 16)
            sp.dma_start(prm[ROW_CW:ROW_CW + 4 * KT, :], conv_w[0].rearrange("j (t p) -> (j t) p", p=P))\
                .then_inc(params_in, 16)

            for t in range(NC):
                sp.dma_start(x_rows[:, t], x_v[:, t]).then_inc(x_rows_in, 16)

            def load(slot, src, split):
                if split is not None:
                    sp.wait_ge(wL_done, split)
                sp.dma_start(w_raw[:, slot, :, 0:src.shape[2]], src).then_inc(w_in_s[slot], 16)

            def pro_load(g):
                n, q = divmod(g, 2)
                off, width = ([(OFF_IF, 2 * NH)] + [(o, P) for o in OFF_SB])[n]
                load(g % 3, w_in_v[:, 4 * q:4 * q + 4, off:off + width], g - 2 if g >= 3 else None)

            for g in range(3):
                pro_load(g)
            for n in range(2 * KT):
                d, what = divmod(n, 2)
                if n >= 3:
                    sp.wait_ge(ada_used, n - 2)
                sp.dma_start(a_raw[:, n % 3], w_ada_v[:, :, what * D + d * P:what * D + (d + 1) * P])\
                    .then_inc(a_in[n % 3], 16)
            for g in range(3, 2 * PRO_JOBS):
                pro_load(g)

            off = dict(zip(("mlq", "mlk", "mlv", "mlo", "mlz"), OFF_ML)) |\
                dict(zip(("sbq", "sbk", "sbv", "sbz"), [o + P for o in OFF_SB]))

            def iteration(i, last):
                fixed = (lambda v: v) if last else sp.snap
                for j, name in enumerate(JOBS_LAST if last else JOBS):
                    start = {"gsb": OFF_GSB, "gml": OFF_GML}.get(name) or fixed(i * P + off[name])
                    for q in range(2):
                        slot, split = (2 * PRO_JOBS + 2 * j + q) % 3, fixed(chunk(i, 2 * j + q) - 2)
                        load(slot, w_in_v[:, 4 * q:4 * q + 4, bass.ds(start, P)], split)

            with sp.Fori(0, NH - 1) as i:
                iteration(i, False)
            iteration(NH - 1, True)

            load((END_CHUNKS + 4) % 3, w_sbp_v[:, :, 0:P], END_CHUNKS + 2)
            load((END_CHUNKS + 5) % 3, w_mlp_v[:, :, 0:P], END_CHUNKS + 3)
            with sp.Fori(1, KT) as m:
                start = [sp.snap(m * P + OFF_GSB), sp.snap(m * P + OFF_GML), sp.snap(m * P)]
                for q, (src, n) in enumerate([(w_in_v[:, 0:4], 0), (w_in_v[:, 4:8], 0), (w_in_v[:, 0:4], 1),
                                              (w_in_v[:, 4:8], 1), (w_sbp_v, 2), (w_mlp_v, 2)]):
                    split = None if q == 4 else sp.snap(m * 6 + (END_CHUNKS + q - 2 + (q == 3)))
                    load((END_CHUNKS + q) % 3, src[:, :, bass.ds(start[n], P)], split)

            sp.wait_ge(filled[1], END_JOBS + 4 * KT)
            sp.dma_start(gate1[:], b_ada[0:1, 2 * D:3 * D].broadcast_to((P, D))).then_inc(bc_in, 16)
            sp.dma_start(lng[:], ln_g[0:1, :].broadcast_to((P, D))).then_inc(bc_in, 16)
            sp.dma_start(lnb[:], ln_b[0:1, :].broadcast_to((P, D))).then_inc(bc_in, 16)
            for q in range(2):
                sp.dma_start(x_in[:, q:q + 1], x_v[:, q:q + 1]).then_inc(x_tile_in[q], 16)

            def pair(r, last):
                fixed = (lambda v: v) if last else sp.snap
                at_ = [fixed(r * 2 + q) for q in range(4)]
                done = [fixed(r * 2 + q + 1) for q in range(2)]
                for q in range(2):
                    sp.wait_ge(out_done, done[q])
                    sp.dma_start(out_v[:, bass.ds(at_[q], 1)], res[:, q:q + 1]).then_inc(stored[q], 16)
                    if not last:
                        sp.dma_start(x_in[:, q:q + 1], x_v[:, bass.ds(at_[2 + q], 1)]).then_inc(x_tile_in[q], 16)

            with sp.Fori(0, NC // 2 - 1) as r:
                pair(r, False)
            pair(NC // 2 - 1, True)
            for q in range(2):
                sp.wait_ge(stored[q], 16 * (NC // 2))

        @block.gpsimd
        def _(pool):
            g = nc.gpsimd
            g.memset(ident[:], 0.0).then_inc(consts, 1)
            g.memset(ones[:], 1.0).then_inc(consts, 1)
            g.memset(sel_all[:], 0.0).then_inc(consts, 1)
            g.memset(upto[:], -1.0).then_inc(consts, 1)
            pool.wait_ge(consts, 4)
            g.affine_select(out=ident[:], in_=ident[:], compare_op=ALU.not_equal, fill=1.0, base=0,
                            pattern=[[-1, P]], channel_multiplier=1).then_inc(consts, 1)
            g.affine_select(out=later[:], in_=ones[:], compare_op=ALU.is_gt, fill=0.0, base=0,
                            pattern=[[1, P]], channel_multiplier=-1).then_inc(consts, 1)
            g.affine_select(out=notbefore[:], in_=ones[:], compare_op=ALU.is_ge, fill=0.0, base=0,
                            pattern=[[1, P]], channel_multiplier=-1).then_inc(consts, 1)
            g.affine_select(out=upto[:], in_=upto[:], compare_op=ALU.is_ge, fill=0.0, base=0,
                            pattern=[[-1, P]], channel_multiplier=1).then_inc(consts, 1)
            g.affine_select(out=sel_all[:], in_=sel_all[:], compare_op=ALU.not_equal, fill=1.0, base=0,
                            pattern=[[-1, NH], [0, P]], channel_multiplier=1).then_inc(consts, 1)
            pool.wait_ge(consts, 9)
            g.affine_select(out=sel_all[:], in_=sel_all[:], compare_op=ALU.not_equal, fill=1.0, base=-32,
                            pattern=[[-1, NH], [0, P]], channel_multiplier=1).then_inc(consts, 1)
            pool.dma_start(r_bias[0:2 * NH, :], b_in[0, OFF_IF:OFF_GSB].rearrange("(p a) -> p a", a=1))\
                .then_inc(bias_in, 16)

            def carry_sums(i, s):
                if closes(s):
                    return
                f = first_col(s)
                for h in range(2):
                    pool.wait_ge(sp_done[h], i * NS + s + 1)
                    if opens(s):
                        pool.wait_ge(ts_zero[h], i * 2 + SLOTS[s][0] + 1)
                    else:
                        pool.wait_ge(tsL_done[h], i * NCAR + carries(s))
                    g.tensor_tensor(tsum[h][:, f:], tsum[h][:, f:], soft[h][:, f:], ALU.add).then_inc(ts_sum[h], 1)
                for h in range(2):
                    pool.wait_ge(tsH_done[h], i * NCAR + carries(s) + 1)
                    g.tensor_tensor(tsL[h][:, f:], tsum[h][:, f:], tsH[h][:, f:], ALU.subtract)\
                        .then_inc(tsL_done[h], 1)

            with pool.Fori(0, NH - 1) as i:
                for s in range(NS):
                    carry_sums(i, s)
            for s in range(NS):
                carry_sums(NH - 1, s)

            for k in range(KT):
                if k == 0:
                    pool.wait_ge(yT_done, 1)
                else:
                    pool.wait_ge(g_acc_step, k)
                pool.dma_start(raw[:], w_ada_v[:, k, 2 * D:3 * D]).then_inc(raw_in, 16)
            for n in range(2 * KT):
                if n < 2:
                    pool.wait_ge(g_acc_step, KT)
                else:
                    pool.wait_ge(woL_done, n - 1)
                pool.dma_start(raw[:, halves(n % 2)], w_out_v[:, n // 2, halves(n % 2)])\
                    .then_inc(wo_in[n % 2], 16)

        @block.tensor
        def _(pe):
            t = nc.tensor

            def split_product(ps, lhs, rhs, k, kt, done=None):
                (aH, aL), (bH, bL) = lhs, rhs
                t.matmul(ps, aH, bH, start=k == 0, stop=False)
                t.matmul(ps, aH, bL, start=False, stop=False)
                return t.matmul(ps, aL, bH, start=False, stop=k == kt - 1)

            def project(i, lo, hi, base_job=None, width=P):
                for n in range(lo, hi):
                    j, r = divmod(n, JOB_MM)
                    half, r = divmod(r, JOB_MM // 2)
                    k, term = divmod(r, 3)
                    number = job(i, j) if base_job is None else base_job + j
                    first = chunk(i, 2 * j) if base_job is None else 2 * (base_job + j)
                    slot0 = (2 * PRO_JOBS + 2 * j if base_job is None else first) % 3
                    if half == 0 and term == 0 and k % 4 == 0:
                        pe.wait_ge(wL_done, first + (k // 4 + 1))
                    if r == 0 and not (base_job == 0):
                        pe.wait_ge(drained[half], number)
                    slot = (slot0 + k // 4) % 3
                    w = (wL if term == 2 else wH)[:, slot, k % 4, 0:width]
                    a = (hL if term == 1 else hH)[:, k, halves(half)]
                    ins = t.matmul(proj_ps[half][0:width, :], w, a, start=(r == 0), stop=(r == JOB_MM // 2 - 1))
                    if r == JOB_MM // 2 - 1:
                        ins.then_inc(filled[half], 1)
                    elif half == 1 and r == 11:
                        ins.then_inc(w_first_used, 1)

            pe.wait_ge(consts, 5)
            pe.wait_ge(params_in, 16 * 7)
            t.transpose(misc_ps[0][:, 0:P], prm[:], ident[:]).then_inc(m_filled[0], 1)
            for f in range(2 * KT):
                half, d = divmod(f, KT)
                n = f % 2
                if d == 0:
                    pe.wait_ge(x_rows_in, 16 * NC)
                if f // 2 + (1 - n) > 0:
                    pe.wait_ge(m_drained[n], f // 2 + (1 - n))
                for q in range(4):
                    ins = t.transpose(misc_ps[n][:, q * P:(q + 1) * P], x_rows[:, 4 * half + q, d * P:(d + 1) * P],
                                      ident[:])
                ins.then_inc(m_filled[n], 1)
            pe.wait_ge(silu_done, 1)
            for n in range(2 * KT):
                d, what = divmod(n, 2)
                pe.wait_ge(a_in[n % 3], 16 * (n // 3 + 1))
                if what == 0 and d >= 2:
                    pe.wait_ge(mod_done, 2 * (d - 1))
                for k in range(KT):
                    ins = t.matmul(z_ps[d % 2][:, what:what + 1], a_raw[:, n % 3, k], silu_c[:, k:k + 1],
                                   start=k == 0, stop=k == KT - 1)
                ins.then_inc(ada_used, 1)

            def gate_columns():
                pe.wait_ge(q_exp, 3)
                for n in range(2):
                    pe.wait_ge(m_drained[n], M_PRO[n] - 1)
                    for q in range(4):
                        cc = 4 * n + q
                        ins = t.transpose(misc_ps[n][:, q * P:(q + 1) * P], r_q[:, cc * P:(cc + 1) * P], ident[:])
                    ins.then_inc(m_filled[n], 1)
                for h in range(NH):
                    ins = t.matmul(misc_ps[2][:, h * NC:(h + 1) * NC], sel_all[32:64, h, :],
                                   r_q[32:64, P - 1:S:P], start=True, stop=True)
                ins.then_inc(m_filled[2], 1)

            for n in range(PRO_JOBS):
                if n == 0:
                    pe.wait_ge(hL_done, KT)
                if n == PRO_JOBS - 1:
                    gate_columns()
                project(0, 0, JOB_MM, base_job=n, width=2 * NH if n == 0 else P)

            def transposes(bank_no, srcs):
                for q, src in enumerate(srcs):
                    ins = t.transpose(misc_ps[bank_no][:, q * P:(q + 1) * P], src, ident[:])
                ins.then_inc(m_filled[bank_no], 1)

            def scores(i, s):
                tc, j = SLOTS[s]
                f = first_col(s)
                for h in range(2):
                    r = slice(64 * h, 64 * h + 64)
                    if s > 0:
                        pe.wait_ge(a_exp[h], i * NS + s)
                    elif h == 0:
                        pe.wait_ge(pair_split, i * 4 + 4)
                    q = slice(tc * HALF + f, (tc + 1) * HALF)
                    kk = slice(j * P, (j + 1) * P)
                    ps = z_ps[h][:, f:]
                    t.matmul(ps, kH[r, kk], qH[r, q], start=True, stop=False)
                    t.matmul(ps, kH[r, kk], qL[r, q], start=False, stop=False)
                    t.matmul(ps, kL[r, kk], qH[r, q], start=False, stop=True).then_inc(z_done[h], 1)

            def exponents(i, s):
                f = first_col(s)
                for h in range(2):
                    if not opens(s):
                        fp = first_col(s - 1)
                        pe.wait_ge(sp_done[h], i * NS + s + 1)
                        pe.wait_ge(tsL_done[h], i * NCAR + carries(s))
                        t.matmul(z_ps[h][:, fp:], neg_ones[:], tsH[h][:, fp:], start=False, stop=False,
                                 skip_group_check=True)
                        t.matmul(z_ps[h][:, fp:], neg_ones[:], tsL[h][:, fp:], start=False, stop=False,
                                 skip_group_check=True)
                    pe.wait_ge(spL_done[h], i * NS + s + 1)
                    t.matmul(z_ps[h][:, f:], neg_upto[:], spH[h][:, f:], start=False, stop=False,
                             skip_group_check=True)
                    t.matmul(z_ps[h][:, f:], neg_upto[:], spL[h][:, f:], start=False, stop=True,
                             skip_group_check=True).then_inc(e_done[h], 1)

            def weighted_values(i, s):
                tc, j = SLOTS[s]
                f = first_col(s)
                if s == 4:
                    pe.wait_ge(y_staged, i * 2 + 1)
                for h in range(2):
                    if diagonal(s):
                        pe.wait_ge(a_mask[h], i * ND + diagonals(s) + 1)
                    else:
                        pe.wait_ge(a_exp[h], i * NS + s + 1)
                    t.matmul(y_ps[64 * h:64 * h + 64, f:], v_tok[:, j, 64 * h:64 * h + 64], soft[h][:, f:],
                             start=opens(s), stop=closes(s), skip_group_check=True).then_inc(pv_done[h], 1)

            def mlstm_first(i, s):
                if s == 0:
                    pe.wait_ge(h_cols, i + 1)
                    for n in range(2):
                        pe.wait_ge(m_drained[n], m_count(n, i, F_R))
                        t.matmul(misc_ps[n][:], sel_cur[0:32, :], bm[0:32, halves(n)], start=True, stop=True)\
                            .then_inc(m_filled[n], 1)
                if s == 3:
                    for n in range(2):
                        pe.wait_ge(m_drained[n], m_count(n, i, F_MV))
                        if n == 0:
                            pe.wait_ge(drained[1], job(i, 2) + 1)
                        transposes(n, [m_vraw[:, cc * P:(cc + 1) * P] for cc in range(4 * n, 4 * n + 4)])
                if s >= 4:
                    cc = s - 4
                    tt = slice(cc * P, (cc + 1) * P)
                    if cc == 0:
                        pe.wait_ge(conv_done, i * 2 + 2)
                    pe.wait_ge(m_drained[0], m_count(0, i, F_CHUNK + cc))
                    if cc == 0:
                        pe.wait_ge(m_drained[1], m_count(1, i, F_CHUNK))
                        pe.wait_ge(state_zero, i + 1)
                    t.matmul(misc_ps[0][:, 0:P], m_k[:, tt], m_q[:, tt], start=True, stop=True)\
                        .then_inc(m_filled[0], 1)
                    pe.wait_ge(m_drained[2], m_count(2, i, cc))
                    t.matmul(misc_ps[2][:, 0:P + 1], m_ktok[:, cc], m_vtok[:, cc], start=True, stop=True)\
                        .then_inc(m_filled[2], 1)
                    pe.wait_ge(m_drained[1], m_count(1, i, F_CHUNK + cc))
                    t.matmul(misc_ps[1][:, 0:P + 1], m_q[:, tt], m_state[:], start=True, stop=True)\
                        .then_inc(qc_done, 1)

            def mlstm_second(i, s):
                if s == 2:
                    for n in range(2):
                        pe.wait_ge(m_drained[n], m_count(n, i, F_MK))
                        if n == 0:
                            pe.wait_ge(conv_done, i * 2 + 1)
                        transposes(n, [m_k[:, cc * P:(cc + 1) * P] for cc in range(4 * n, 4 * n + 4)])
                if s >= 4:
                    cc = s - 4
                    pe.wait_ge(m_drained[0], m_count(0, i, F_CHUNK + cc) + 1)
                    t.matmul(misc_ps[1][:, 2 * P:3 * P + 1], m_s[:], m_vtok[:, cc], start=True, stop=True)\
                        .then_inc(m_filled[1], 1)

            def iteration(i, last):
                segs, end = segments(last)
                project(i, 0, 24)
                for n in range(2):
                    pe.wait_ge(m_drained[n], m_count(n, i, F_V))
                    if n == 0:
                        pe.wait_ge(drained[1], job(i, -2) + 1)
                    transposes(n, [next_v[:, cc * P:(cc + 1) * P] for cc in range(4 * n, 4 * n + 4)])
                project(i, 24, PRE)
                for s in range(NS):
                    a, b, c_, d = segs[s]
                    scores(i, s)
                    if s > 0:
                        weighted_values(i, s - 1)
                    else:
                        pe.wait_ge(m_drained[1], m_count(1, i, F_V) + 1)
                    project(i, a, b)
                    mlstm_first(i, s)
                    project(i, b, c_)
                    mlstm_second(i, s)
                    exponents(i, s)
                    project(i, c_, d)
                project(i, segs[-1][3], end)
                weighted_values(i, NS - 1)
                for n in range(2):
                    pe.wait_ge(hn_done, i * NC + 4 * n + 4)
                    pe.wait_ge(m_drained[n], m_count(n, i, F_HN))
                    transposes(n, [m_num[:, cc, 0:P] for cc in range(4 * n, 4 * n + 4)])

            with pe.Fori(0, NH - 1) as i:
                iteration(i, False)
            iteration(NH - 1, True)

            def merge_tile(m, first):
                for r in range(2 if first else 0, 4):
                    kt = KT if r < 2 else NH
                    for half in range(2):
                        pe.wait_ge(drained[half], m * 4 + (END_JOBS + r))
                        for k in range(kt):
                            g_ = (0, 2, 4, 5)[r] + k // 4
                            if half == 0 and k % 4 == 0:
                                pe.wait_ge(wL_done, m * 6 + (END_CHUNKS + g_ + 1))
                            if first and r >= 2 and half == 0 and k == 0:
                                pe.wait_ge(yb_L, NH * (r - 1))
                            slot = (END_CHUNKS + g_) % 3
                            a = (hH, hL) if r < 2 else (ybH[r - 2], ybL[r - 2])
                            ins = split_product(proj_ps[half][:], (wH[:, slot, k % 4], wL[:, slot, k % 4]),
                                                [z[:, k, halves(half)] for z in a], k, kt)
                            if r < 2 and half == 1 and k == 3:
                                ins.then_inc(w_first_used, 1)
                        ins.then_inc(filled[half], 1)

            merge_tile(0, True)
            with pe.Fori(1, KT) as m:
                merge_tile(m, False)

            pe.wait_ge(g_acc_step, KT)
            for n in range(2):
                pe.wait_ge(m_drained[n], m_count(n, NH, 0))
                t.matmul(misc_ps[n][:], ones[:], g_acc[:, halves(n)], start=True, stop=True)\
                    .then_inc(m_filled[n], 1)

            pe.wait_ge(woL_done, 2 * KT)

            def out_tile(r, q):
                pe.wait_ge(yL_done, r * 2 + q + 1)
                for half in range(2):
                    pe.wait_ge(drained[half], r * 2 + (END_JOBS + 4 * KT + q))
                    for k in range(KT):
                        ins = split_product(proj_ps[half][:], (yH[:, q, k], yL[:, q, k]),
                                            (hH[:, k, halves(half)], hL[:, k, halves(half)]), k, KT)
                    ins.then_inc(filled[half], 1)

            with pe.Fori(0, NC // 2) as r:
                for q in range(2):
                    out_tile(r, q)

        @block.scalar
        def _(act):
            a = nc.scalar
            a.preload_act_table_set("natural_log_exp_and_others")

            for f in range(0, 2 * KT, 2):
                half, d = divmod(f, KT)
                act.wait_ge(m_filled[0], f // 2 + 2)
                a.activation(xT[:, d, halves(half)], misc_ps[0][:], ACT.Copy).then_inc(m_drained[0], 1)
                if f == 0:
                    act.wait_ge(cols_done, 1)
                    a.activation(small[:, 0:KT], cols[:, ROW_C:ROW_C + KT], ACT.Exp, scale=-1.0).then_inc(c_exp, 1)

            def split_high(slot, loads, freed, scale=1.0, width=P):
                act.wait_ge(w_in_s[slot], loads)
                if freed is not None:
                    act.wait_ge(*freed)
                a.activation(wH[:, slot, :, 0:width], w_raw[:, slot, :, 0:width], ACT.Copy, scale=scale)\
                    .then_inc(wH_done, 1)

            def pro_split(g):
                n = g // 2
                freed = None
                if g >= 3:
                    n3, odd = divmod(g - 3, 2)
                    freed = (filled[1] if odd else w_first_used, n3 + 1)
                split_high(g % 3, 16 * (g // 3 + 1), freed, SB_SCALE if n == 1 else 1.0, 2 * NH if n == 0 else P)

            for g in range(3):
                pro_split(g)
            for d in range(KT):
                act.wait_ge(h_full, d + 1)
                a.activation(hH[:, d], xT[:, d], ACT.Copy).then_inc(hH_done, 1)

            def bias_copy(dst, half, number, bias, rows=P):
                act.wait_ge(filled[half], number + 1)
                a.activation(dst, proj_ps[half][0:rows, :], ACT.Identity, bias=bias, scale=1.0)\
                    .then_inc(drained[half], 1)

            def exp_into_sig(dst, half, number, bias, nbias, used=None):
                act.wait_ge(filled[half], number + 1)
                if used is not None:
                    act.wait_ge(sig_used, used)
                a.activation(sig[:, halves(half)], proj_ps[half][:], ACT.Exp, bias=nbias, scale=-1.0)\
                    .then_inc(sig_exp, 1)
                a.activation(dst[:, halves(half)], proj_ps[half][:], ACT.Identity, bias=bias, scale=1.0)\
                    .then_inc(drained[half], 1)

            for n in range(PRO_JOBS):
                for half in range(2):
                    if n == 0:
                        if half == 0:
                            act.wait_ge(bias_in, 16)
                            act.wait_ge(rows_zero, 1)
                        bias_copy(r_if[0:2 * NH, halves(half)], half, n, r_bias[0:2 * NH, :], 2 * NH)
                    elif n < 4:
                        b = cols[:, 4 * (n - 1):4 * (n - 1) + 1]
                        bias_copy((next_q, next_k, next_v)[n - 1][:, halves(half)], half, n, b)
                    else:
                        exp_into_sig(next_g, half, n, cols[:, 12:13], ncols[:, 12:13])
                    g = 2 * n + 3 + half
                    if g < 2 * PRO_JOBS + 2:
                        if g >= 2 * PRO_JOBS:
                            n3, odd = divmod(g - 3, 2)
                            split_high(g % 3, 16 * (g // 3 + 1), (filled[1] if odd else w_first_used, n3 + 1))
                        else:
                            pro_split(g)
                if n == 0:
                    act.wait_ge(drained[1], 1)
                    for q in range(4):
                        act.dma_start(r_i[32 * q:32 * q + NH, :], r_if[0:NH, :]).then_inc(rows_in, 16)
                        act.dma_start(r_f[32 * q:32 * q + NH, :], r_if[NH:2 * NH, :]).then_inc(rows_in, 16)
                if n == 1:
                    act.wait_ge(rows_in, 16 * 8)
                    a.activation(r_e[:], r_f[:], ACT.Exp, scale=-1.0).then_inc(f_ln, 1)
                    act.wait_ge(f_ln, 1)
                    a.activation(r_e[:], r_e[:], ACT.Ln, bias=1.0).then_inc(f_ln, 1)
                if n == 2:
                    for q in range(1, 4):
                        r = slice(32 * q, 32 * q + 32)
                        act.wait_ge(q_rows, q)
                        a.activation(r_q[r, :], r_q[r, :], ACT.Exp).then_inc(q_exp, 1)

            def softplus_logs(i, s):
                f = first_col(s)
                for h in range(2):
                    act.wait_ge(z_done[h], i * NS + s + 1)
                    if s > 0:
                        act.wait_ge(pv_done[h], i * NS + s)
                    a.activation(soft[h][:, f:], z_ps[h][:, f:], ACT.Exp).then_inc(ex_done[h], 1)
                for h in range(2):
                    act.wait_ge(ex_done[h], i * NS + s + 1)
                    a.activation(soft[h][:, f:], soft[h][:, f:], ACT.Ln, bias=1.0).then_inc(ln_done[h], 1)

            def softplus_high(i, s):
                f = first_col(s)
                for h in range(2):
                    act.wait_ge(sp_done[h], i * NS + s + 1)
                    a.activation(spH[h][:, f:], soft[h][:, f:], ACT.Copy).then_inc(spH_done[h], 1)

            def attention_weights(i, s):
                f = first_col(s)
                for h in range(2):
                    act.wait_ge(e_done[h], i * NS + s + 1)
                    if not closes(s):
                        act.wait_ge(ts_sum[h], i * NCAR + carries(s) + 1)
                    a.activation(soft[h][:, f:], z_ps[h][:, f:], ACT.Exp).then_inc(a_exp[h], 1)

            def store_y(i, tc):
                act.wait_ge(y_staged, i * 2 + tc + 1)
                dst = ysb_dram[i] if isinstance(i, int) else ysb_dram[bass.ds(i, 1)].rearrange("a p s -> (a p) s")
                act.dma_start(dst[:, halves(tc)], y_stage[:]).then_inc(y_stored, 16)

            def tasks(i, lo, hi, last):
                for what, n, half in events(lo, hi, last):
                    if what == "split":
                        cc = n
                        j3, odd = divmod(cc - 3, 2)
                        scale = SB_SCALE if (not last and cc // 2 < NJ and JOBS[cc // 2] == "sbq") else 1.0
                        slot = (2 * PRO_JOBS + cc) % 3
                        loads = i * (16 * 2 * NJ // 3) + 16 * ((2 * PRO_JOBS + cc) // 3 + 1)
                        split_high(slot, loads, (filled[1] if odd else w_first_used, job(i, j3) + 1), scale)
                        continue
                    if what == "o_log":
                        act.wait_ge(o_capped, i + 1)
                        a.activation(m_gate[:], m_gate[:], ACT.Ln, bias=1.0).then_inc(o_log, 1)
                        continue
                    if what == "z_log":
                        act.wait_ge(sig_capped, i * 2 + 2)
                        a.activation(sig[:], sig[:], ACT.Ln, bias=1.0).then_inc(sig_log, 1)
                        continue
                    if what == "z_exp":
                        act.wait_ge(z_sum, i + 1)
                        a.activation(sig[:], sig[:], ACT.Exp, scale=-1.0).then_inc(sig_done, 1)
                        continue
                    if what == "z_mul":
                        continue
                    name, number = (JOBS_LAST if last else JOBS)[n], job(i, n)
                    if name in ("gsb", "gml"):
                        dst, row = {"gsb": (sigs, ROW_GSB), "gml": (sigm, ROW_GML)}[name]
                        if half == 0:
                            act.wait_ge(pair_split, i * 4 + 4)
                        act.wait_ge(filled[half], number + 1)
                        a.activation(dst[:, halves(half)], proj_ps[half][:], ACT.Exp, bias=ncols[:, row:row + 1],
                                     scale=-1.0).then_inc(drained[half], 1)
                    elif name == "mlv":
                        bias_copy(m_vraw[:, halves(half)], half, number, bias_of(name))
                    elif name in ("mlk", "mlq"):
                        if name == "mlk" and half == 0:
                            act.wait_ge(h_cols, i + 1)
                        if name == "mlq" and half == 0:
                            act.wait_ge(conv_acc, i * 4 + 2)
                        bias_copy(conv_in[:, 3 + half * HALF:3 + (half + 1) * HALF], half, number, bias_of(name))
                    elif name == "mlo":
                        act.wait_ge(filled[half], number + 1)
                        if half == 0:
                            act.wait_ge(m_drained[1], m_count(1, i, 0))
                        a.activation(m_gate[:, halves(half)], proj_ps[half][:], ACT.Exp,
                                     bias=bias_of(name, True), scale=-1.0).then_inc(drained[half], 1)
                    elif name == "mlz":
                        exp_into_sig(m_vraw, half, number, bias_of(name), bias_of(name, True), i * 2 + 1)
                    elif name == "sbz":
                        exp_into_sig(next_g, half, number, bias_of(name), bias_of(name, True), i * 2 + 2)
                    else:
                        if half == 0:
                            act.wait_ge(pair_split, i * 4 + 4)
                            if name == "sbv":
                                act.wait_ge(m_filled[1], m_count(1, i, F_V) + 1)
                        dst = {"sbq": next_q, "sbk": next_k, "sbv": next_v}[name]
                        bias_copy(dst[:, halves(half)], half, number, bias_of(name))

            by_chunk = lambda z: z.rearrange("p (c t) -> p c t", t=P)

            def conv_exps(i, k):
                act.wait_ge(conv_acc, i * 4 + 2 * k + 2)
                if k:
                    act.wait_ge(conv_done, i * 2 + 1)
                a.activation(m_num[:, :, 0:P], by_chunk((m_k, m_q)[k][:]), ACT.Exp, scale=-1.0).then_inc(conv_exp, 1)

            def conv_sigmoid(i, k):
                act.wait_ge(conv_cap, i * 2 + k + 1)
                a.activation(m_num[:, :, 0:P], m_num[:, :, 0:P], ACT.Ln, bias=1.0).then_inc(conv_log, 1)
                act.wait_ge(conv_log, i * 2 + k + 1)
                a.activation(m_num[:, :, 0:P], m_num[:, :, 0:P], ACT.Exp, scale=-1.0).then_inc(conv_sig, 1)

            def token_major(i, bank_fill, dst):
                for n in range(2):
                    act.wait_ge(m_filled[n], m_count(n, i, bank_fill) + 1)
                    a.activation(dst[:, 4 * n:4 * n + 4, 0:P], misc_ps[n][:].rearrange("p (a b) -> p a b", a=4),
                                 ACT.Copy).then_inc(m_drained[n], 1)

            def place0(i, s):
                if s == 4:
                    store_y(i, 0)
                if s == 3:
                    conv_sigmoid(i, 1)

            def place1(i, s):
                if s == 0:
                    act.wait_ge(w_sum, i + 1)
                    a.activation(m_w[:], m_w[:], ACT.Exp).then_inc(w_exp, 1)
                    conv_exps(i, 0)
                if s == 1:
                    conv_sigmoid(i, 0)
                if s == 2:
                    conv_exps(i, 1)
                if s == 3:
                    token_major(i, F_MV, m_vtok)

            def iteration(i, last):
                segs, end = segments(last)
                act.wait_ge(sig_capped, i * 2 + 1)
                a.activation(sig[:], sig[:], ACT.Ln, bias=1.0).then_inc(sig_log, 1)
                tasks(i, -1, 24, last)
                token_major(i, F_V, v_tok)
                act.wait_ge(sig_log, i * 2 + 1)
                a.activation(sig[:], sig[:], ACT.Exp, scale=-1.0).then_inc(sig_done, 1)
                tasks(i, 24, PRE, last)
                for s in range(NS):
                    p0, p1, p2, p3 = segs[s]
                    softplus_logs(i, s)
                    tasks(i, p0, p1, last)
                    place0(i, s)
                    softplus_high(i, s)
                    tasks(i, p1, p2, last)
                    place1(i, s)
                    attention_weights(i, s)
                    tasks(i, p2, p3, last)
                act.wait_ge(var_done, i + 1)
                a.activation(small[:, 24:32], small[:, 16:24], ACT.Ln, bias=EPS).then_inc(rstd_ln, 1)
                act.wait_ge(rstd_ln, i + 1)
                a.activation(small[:, 24:32], small[:, 24:32], ACT.Exp, scale=-0.5).then_inc(rstd_exp, 1)
                tasks(i, segs[-1][3], end, last)
                store_y(i, 1)
                for n in range(2):
                    act.wait_ge(m_drained[n], m_count(n, i, F_HN) + 1)
                dst = yml_dram[i] if isinstance(i, int) else yml_dram[bass.ds(i, 1)].rearrange("a p s -> (a p) s")
                act.dma_start(dst, m_w[:].rearrange("p a b -> p (a b)")).then_inc(yml_stored, 16)

            with act.Fori(0, NH - 1) as i:
                iteration(i, False)
            iteration(NH - 1, True)

            act.wait_ge(y_stored, 16 * (2 * NH + 1))
            act.wait_ge(yml_stored, 16 * (NH + 1))
            act.wait_ge(drained[1], END_JOBS)
            for b, src in enumerate((ysb_dram, yml_dram)):
                for p in range(NH):
                    act.dma_start(yT[:, NH * b + p], src[p]).then_inc(y_in[b], 16)

            def merge_split(m, q):
                g = END_CHUNKS + q
                freed = {2: (filled[1], m * 4 + END_JOBS), 3: (w_first_used, m * 2 + (END_JOBS + 1)),
                         4: (filled[1], m * 4 + (END_JOBS + 1)), 5: (w_first_used, m * 2 + (END_JOBS + 2)),
                         6: (filled[1], m * 4 + (END_JOBS + 2)), 7: (filled[1], m * 4 + (END_JOBS + 3)),
                         8: (filled[1], m * 4 + (END_JOBS + 4))}[q]
                split_high(g % 3, m * 32 + 16 * (g // 3 + 1), freed)

            def gate_sigmoid(m, r):
                z = (sigs, sigm)[r]
                act.wait_ge(g_capped[r], m + 1)
                a.activation(z[:], z[:], ACT.Ln, bias=1.0).then_inc(g_log[r], 1)
                act.wait_ge(g_log[r], m + 1)
                a.activation(z[:], z[:], ACT.Exp, scale=-1.0).then_inc(g_done[r], 1)

            def merge_tile(m, first, last):
                for r in range(2):
                    for half in range(0 if first else 2):
                        if r == 0 or half == 0:
                            act.wait_ge(drained[half], m * 4 + (END_JOBS + r - 1))
                        act.wait_ge(filled[half], m * 4 + (END_JOBS + r + 1))
                        if half:
                            merge_split(m, 3 + 2 * r)
                        row = (ROW_GSB, ROW_GML)[r]
                        a.activation((sigs, sigm)[r][:, halves(half)], proj_ps[half][:], ACT.Exp,
                                     bias=ncols[:, bass.ds(m + row, 1)], scale=-1.0).then_inc(drained[half], 1)
                        if half and not (last and r):
                            merge_split(m, 4 + 2 * r)
                    if first:
                        act.wait_ge(y_in[r], 16 * NH)
                        for p in range(NH):
                            a.activation(ybH[r][:, p], yT[:, NH * r + p], ACT.Copy).then_inc(yb_H, 1)
                        if r == 0:
                            merge_split(m, 6)
                    gate_sigmoid(m, r)
                if not last:
                    merge_split(m, 7)
                    merge_split(m, 8)

            merge_tile(0, True, False)
            with act.Fori(1, KT - 1) as m:
                merge_tile(m, False, False)
            merge_tile(KT - 1, False, True)
            for n in range(2 * KT):
                act.wait_ge(wo_in[n % 2], 16 * (n // 2 + 1))
                if n == 0:
                    act.wait_ge(filled[1], END_JOBS + 4 * (KT - 1) + 2)
                a.activation(hH[:, n // 2, halves(n % 2)], raw[:, halves(n % 2)], ACT.Copy).then_inc(woH_done, 1)

            def y_high(r, q, free):
                if free is not None:
                    act.wait_ge(filled[1], free)
                src = yT[:, :, bass.ds(r * 2 * P + q * P, P)]
                a.activation(yH[:, q], src, ACT.Copy).then_inc(yH_done, 1)

            def rstd(r, q):
                c0 = 8 * q
                act.wait_ge(var_done, r * 2 + (NH + q + 1))
                a.activation(small[:, c0 + 2:c0 + 3], small[:, c0 + 1:c0 + 2], ACT.Ln, bias=EPS).then_inc(rstd_ln, 1)
                act.wait_ge(rstd_ln, r * 2 + (NH + q + 1))
                a.activation(small[:, c0 + 2:c0 + 3], small[:, c0 + 2:c0 + 3], ACT.Exp, scale=-0.5)\
                    .then_inc(rstd_exp, 1)

            act.wait_ge(yT_done, 2 * KT + 1)
            act.wait_ge(filled[1], END_JOBS + 4 * KT)
            y_high(0, 0, None)
            y_high(0, 1, None)

            def out_pair(r, last):
                for q in range(2):
                    if not last:
                        y_high(r + 1, q, r * 2 + (END_JOBS + 4 * KT + q + 1))
                    rstd(r, q)

            with act.Fori(0, NC // 2 - 1) as r:
                out_pair(r, False)
            out_pair(NC // 2 - 1, True)

        @block.vector
        def _(dve):
            v = nc.vector
            link = Chain(dve, dve_step)
            credit = 16

            dve.wait_ge(consts, 10)
            v.tensor_copy(neg_upto[:], upto[:]).then_inc(consts_r, 1)
            v.tensor_scalar(neg_ones[:], ones[:], -1.0, None, ALU.mult).then_inc(consts_r, 1)
            dve.wait_ge(m_filled[0], 1)
            link(v.tensor_copy(cols[:], misc_ps[0][:, 0:P]))
            link(v.tensor_scalar(cols[:, 0:4], cols[:, 0:4], SB_SCALE, None, ALU.mult))
            v.tensor_scalar(ncols[:], cols[:], -1.0, None, ALU.mult).then_inc(m_drained[0], 1)
            dve.wait_ge(m_drained[0], 1)
            dve.sem_inc(cols_done, 1)
            dve.wait_ge(c_exp, 1)
            link(v.tensor_scalar(small[:, 0:KT], small[:, 0:KT], 1.0, None, ALU.add))
            link(v.reciprocal(small[:, 8:16], small[:, 0:KT]))
            v.tensor_tensor(silu_c[:], cols[:, ROW_C:ROW_C + KT], small[:, 8:16], ALU.mult).then_inc(silu_done, 1)
            for f in range(1, 2 * KT, 2):
                half, d = divmod(f, KT)
                dve.wait_ge(m_filled[1], f // 2 + 1)
                v.tensor_copy(xT[:, d, halves(half)], misc_ps[1][:]).then_inc(m_drained[1], 1)

            def split_low(slot, number, scale=1.0, width=P):
                dve.wait_ge(wH_done, number)
                v.scalar_tensor_tensor(out=wL[:, slot, :, 0:width], in0=w_raw[:, slot, :, 0:width], scalar=scale,
                                       in1=wH[:, slot, :, 0:width], op0=ALU.mult, op1=ALU.subtract)\
                    .then_inc(wL_done, 1)

            def pro_split(g):
                n = g // 2
                split_low(g % 3, g + 1, SB_SCALE if n == 1 else 1.0, 2 * NH if n == 0 else P)

            for g in range(3):
                pro_split(g)

            def low_h(d):
                dve.wait_ge(hH_done, d + 1)
                v.tensor_tensor(hL[:, d], xT[:, d], hH[:, d], ALU.subtract).then_inc(hL_done, 1)

            dve.wait_ge(m_drained[0], 9)
            for d in range(KT):
                dve.wait_ge(ada_used, 2 * d + 2)
                z = z_ps[d % 2]
                v.tensor_scalar(mod[:, 0, d:d + 1], z[:, 0:1], cols[:, ROW_ADA + d:ROW_ADA + d + 1], None, ALU.add)\
                    .then_inc(mod_done, 1)
                v.tensor_scalar(mod[:, 1, d:d + 1], z[:, 1:2], cols[:, ROW_ADA + KT + d:ROW_ADA + KT + d + 1], 1.0,
                                ALU.add, ALU.add).then_inc(mod_done, 1)
                dve.wait_ge(mod_done, 2 * d + 2)
                if d == 0:
                    dve.wait_ge(m_drained[1], 8)
                v.tensor_scalar(xT[:, d], xT[:, d], mod[:, 1, d:d + 1], mod[:, 0, d:d + 1], ALU.mult, ALU.add)\
                    .then_inc(h_full, 1)
                if d:
                    low_h(d - 1)
            low_h(KT - 1)

            def row_logs():
                dve.wait_ge(f_ln, 2)
                link(v.tensor_scalar(r_e[:], r_e[:], -1.0, -SOFT_CAP, ALU.mult, ALU.max))
                link(v.tensor_tensor(r_f[:], r_f[:], r_e[:], ALU.min))
                v.tensor_tensor_scan(r_b[:], r_one[:], r_f[:], 0.0, ALU.mult, ALU.add).then_inc(dve_step, 1)
                link.k += 1
                link(v.tensor_tensor_scan(r_m[:], r_f[:], r_i[:], 0.0, ALU.add, ALU.max))
                v.tensor_tensor(bm[:], r_b[:], r_m[:], ALU.subtract).then_inc(dve_step, 1)
                link.k += 1
                link(v.tensor_tensor(r_e[:], r_i[:], r_b[:], ALU.subtract))
                by = lambda z: z.rearrange("p (c t) -> p c t", t=P)
                v.tensor_copy(r_q[0:32, :], r_e[0:32, :]).then_inc(tok_done, 1)
                r = slice(32, 64)
                v.tensor_copy(r_q[r, 0:P], bm[r, 0:P]).then_inc(tok_done, 1)
                before = by(r_m[r, :])[:, 0:NC - 1, P - 1:P].to_broadcast((32, NC - 1, P))
                v.tensor_tensor(by(r_q[r, :])[:, 1:NC], by(bm[r, :])[:, 1:NC], before, ALU.add).then_inc(q_rows, 1)
                r = slice(64, 96)
                v.tensor_scalar(r_q[r, :], r_m[r, :], -1.0, None, ALU.mult).then_inc(q_rows, 1)
                r = slice(96, 128)
                ends = by(bm[r, :])[:, :, P - 1:P].to_broadcast((32, NC, P))
                v.tensor_tensor(by(r_q[r, :]), by(r_e[r, :]), ends, ALU.add).then_inc(q_rows, 1)

            for n in range(PRO_JOBS):
                if n == 0:
                    dve.wait_ge(hL_done, KT)
                    for z in (r_i, r_f, r_if):
                        link(v.memset(z[:], 0.0))
                    link(v.memset(r_one[:], 1.0))
                    v.memset(r_one[:, 0:S:P], 0.0).then_inc(dve_step, 1)
                    link.k += 1
                    dve.wait_ge(dve_step, link.base + link.k)
                    dve.sem_inc(rows_zero, 1)
                for half in range(2):
                    g = 2 * n + 3 + half
                    if g < 2 * PRO_JOBS:
                        pro_split(g)
                    elif g < 2 * PRO_JOBS + 2:
                        split_low(g % 3, g + 1)
                if n == 2:
                    row_logs()
                if n == 3:
                    for b in range(2):
                        dve.wait_ge(m_filled[b], M_PRO[b])
                        src = misc_ps[b][:].rearrange("p (c q r) -> p c q r", c=4, q=4)[:, :, :, 0:NH]
                        v.tensor_copy(tok[:, 4 * b:4 * b + 4], src).then_inc(m_drained[b], 1)
                    dve.wait_ge(m_filled[2], 1)
                    v.tensor_copy(dec[:].rearrange("p c h -> p h c"),
                                  misc_ps[2][:, 0:NH * NC].rearrange("p (h c) -> p h c", h=NH))\
                        .then_inc(m_drained[2], 1)
            dve.wait_ge(m_drained[2], 1)
            v.memset(conv_in[:, 0:3], 0.0).then_inc(conv_pad, 1)
            v.memset(m_vtok[:, :, P:P + 1], 1.0).then_inc(conv_pad, 1)
            dve.sem_inc(y_stored, credit)
            dve.sem_inc(yml_stored, credit)
            link.base, link.k = link.base + link.k, 0

            def head_columns(i, last):
                dve.wait_ge(drained[1], job(i, 0))
                grp = cols[:, 0:36].rearrange("p (g h) -> p g h", h=NH)
                one = lambda lo: cols[:, bass.ds(i + lo, 1)]
                v.tensor_copy(h_col[:, 0:9], grp[:, :, bass.ds(i, 1)].rearrange("p g a -> p (g a)"))\
                    .then_inc(dve_step, 1)
                n = 1
                if not last:
                    v.tensor_copy(h_col[:, 9:18], grp[:, :, bass.ds(i + 1, 1)].rearrange("p g a -> p (g a)"))\
                        .then_inc(dve_step, 1)
                    n += 1
                taps = cols[:, ROW_CW:ROW_CW + 32].rearrange("p (j t) -> p j t", t=2 * NH)
                for which, lo in (("q", 0), ("k", NH)):
                    at_ = H_TAP[which]
                    v.tensor_copy(h_col[:, at_:at_ + 4], taps[:, :, bass.ds(i + lo, 1)].rearrange("p g a -> p (g a)"))\
                        .then_inc(dve_step, 1)
                    v.tensor_copy(h_col[:, H_CB[which]:H_CB[which] + 1], one(ROW_CB + lo)).then_inc(dve_step, 1)
                    n += 2
                v.tensor_copy(h_col[:, H_NG:H_NG + 1], one(ROW_NG)).then_inc(dve_step, 1)
                v.tensor_copy(h_tok[:], tok[:, :, :, bass.ds(i, 1)].rearrange("p c q a -> p q (c a)"))\
                    .then_inc(dve_step, 1)
                v.tensor_copy(h_dec[:], dec[:, :, bass.ds(i, 1)].rearrange("p c a -> p (c a)")).then_inc(dve_step, 1)
                n += 3
                link.k += n
                link(v.tensor_copy(sel_cur[:], sel_all[:, bass.ds(i, 1), :].rearrange("p a b -> p (a b)")))
                width = 9 if last else 18
                v.tensor_scalar(h_col[:, H_NEG:H_NEG + width], h_col[:, 0:width], -1.0, None, ALU.mult)\
                    .then_inc(h_cols, 1)
                v.memset(m_state[:], 0.0).then_inc(state_zero, 1)

            def split_pair(i):
                dve.wait_ge(drained[1], job(i, -3) + 1)
                for n, (src, hi, lo) in enumerate(((next_k, kH, kL), (next_q, qH, qL))):
                    v.tensor_copy(hi[:], src[:]).then_inc(pair_split, 1)
                    dve.wait_ge(pair_split, i * 4 + (2 * n + 1))
                    v.tensor_tensor(lo[:], src[:], hi[:], ALU.subtract).then_inc(pair_split, 1)

            def sum_zero(i, s):
                if opens(s):
                    for h in range(2):
                        if s > 0:
                            dve.wait_ge(tsL_done[h], i * NCAR + carries(s))
                        v.memset(tsum[h][:], 0.0).then_inc(ts_zero[h], 1)

            def softplus(i, s):
                f = first_col(s)
                for h in range(2):
                    dve.wait_ge(ln_done[h], i * NS + s + 1)
                    v.scalar_tensor_tensor(out=soft[h][:, f:], in0=soft[h][:, f:], scalar=SOFT_CAP, in1=z_ps[h][:, f:],
                                           op0=ALU.min, op1=ALU.max)\
                        .then_inc(sp_raw[h] if diagonal(s) else sp_done[h], 1)
                if diagonal(s):
                    for h in range(2):
                        dve.wait_ge(sp_raw[h], i * ND + diagonals(s) + 1)
                        d = soft[h][:, f:f + P]
                        v.tensor_tensor(d, d, later[:], ALU.mult).then_inc(sp_done[h], 1)

            def softplus_low(i, s):
                f = first_col(s)
                for h in range(2):
                    dve.wait_ge(spH_done[h], i * NS + s + 1)
                    v.tensor_tensor(spL[h][:, f:], soft[h][:, f:], spH[h][:, f:], ALU.subtract)\
                        .then_inc(spL_done[h], 1)

            def carry_high(i, s):
                if closes(s):
                    return
                f = first_col(s)
                for h in range(2):
                    dve.wait_ge(ts_sum[h], i * NCAR + carries(s) + 1)
                    dve.wait_ge(e_done[h], i * NS + s + 1)
                    v.tensor_copy(tsH[h][:, f:], tsum[h][:, f:]).then_inc(tsH_done[h], 1)

            def mask_weights(i, s):
                if not diagonal(s):
                    return
                f = first_col(s)
                for h in range(2):
                    dve.wait_ge(a_exp[h], i * NS + s + 1)
                    d = soft[h][:, f:f + P]
                    v.scalar_tensor_tensor(out=d, in0=d, scalar=3.0e38, in1=later[:], op0=ALU.min, op1=ALU.mult)\
                        .then_inc(a_mask[h], 1)

            def gate_y(i, tc):
                for h in range(2):
                    dve.wait_ge(pv_done[h], i * NS + (4 if tc == 0 else NS))
                dve.wait_ge(y_stored, i * 32 + (credit + 16 * tc))
                v.tensor_tensor(y_stage[:], y_ps[:], g_cur[:, halves(tc)], ALU.mult).then_inc(y_staged, 1)

            def tasks(i, lo, hi, last):
                for what, n, half in events(lo, hi, last):
                    if what == "split":
                        scale = SB_SCALE if (not last and n // 2 < NJ and JOBS[n // 2] == "sbq") else 1.0
                        split_low((2 * PRO_JOBS + n) % 3, chunk(i, n) + 1, scale)
                        continue
                    if what == "o_log":
                        for h in range(2):
                            dve.wait_ge(drained[h], job(i, 3) + 1)
                        v.tensor_scalar(m_gate[:], m_gate[:], EXP_CAP, None, ALU.min).then_inc(o_capped, 1)
                    elif what == "z_log":
                        cap_sig(i * 2 + 1)
                    elif what == "z_exp":
                        dve.wait_ge(sig_log, i * 2 + 2)
                        dve.wait_ge(o_log, i + 1)
                        v.tensor_tensor(sig[:], sig[:], m_gate[:], ALU.add).then_inc(z_sum, 1)
                    elif what == "z_mul":
                        dve.wait_ge(drained[1], job(i, 4) + 1)
                        dve.wait_ge(sig_done, i * 2 + 2)
                        v.tensor_tensor(m_gate[:], sig[:], m_vraw[:], ALU.mult).then_inc(sig_used, 1)
                        dve.wait_ge(sig_used, i * 2 + 2)
                        dve.sem_inc(m_gate_done, 1)

            def cap_sig(use):
                dve.wait_ge(sig_exp, use * 2 + 2)
                v.tensor_scalar(sig[:], sig[:], EXP_CAP, None, ALU.min).then_inc(sig_capped, 1)

            def pair_gate(i):
                dve.wait_ge(sig_done, i * 2 + 1)
                v.tensor_tensor(g_cur[:], next_g[:], sig[:], ALU.mult).then_inc(sig_used, 1)
                dve.wait_ge(sig_used, i * 2 + 1)

            def conv_sum(i, k):
                which, half = ("k", "q")[k // 2], k % 2
                dst = (m_k, m_q)[k // 2][:, halves(half)]
                tap = lambda j: h_col[:, H_TAP[which] + j:H_TAP[which] + j + 1]
                src = lambda j: conv_in[:, half * HALF + j:half * HALF + j + HALF]
                dve.wait_ge(drained[half], job(i, k // 2) + 1)
                link(v.tensor_scalar(dst, src(3), tap(3), h_col[:, H_CB[which]:H_CB[which] + 1], ALU.mult, ALU.add))
                for j in (2, 1):
                    link(v.scalar_tensor_tensor(out=dst, in0=src(j), scalar=tap(j), in1=dst, op0=ALU.mult,
                                                op1=ALU.add))
                v.scalar_tensor_tensor(out=dst, in0=src(0), scalar=tap(0), in1=dst, op0=ALU.mult, op1=ALU.add)\
                    .then_inc(conv_acc, 1)

            def conv_bound(i, k):
                dve.wait_ge(conv_exp, i * 2 + k + 1)
                v.tensor_scalar(m_num[:, :, 0:P], m_num[:, :, 0:P], EXP_CAP, None, ALU.min).then_inc(conv_cap, 1)

            def conv_silu(i, k):
                dst = (m_k, m_q)[k][:].rearrange("p (c t) -> p c t", t=P)
                dve.wait_ge(conv_sig, i * 2 + k + 1)
                v.scalar_tensor_tensor(out=dst, in0=m_num[:, :, 0:P], scalar=ML_SCALE if k else 1.0, in1=dst,
                                       op0=ALU.mult, op1=ALU.mult).then_inc(conv_done, 1)

            def chunk_weights(i):
                dve.wait_ge(yml_stored, i * 16 + credit)
                for n in range(2):
                    dve.wait_ge(m_filled[n], m_count(n, i, F_R) + 1)
                    u = h_tok[:, 0, 4 * n:4 * n + 4].unsqueeze(2).to_broadcast((P, 4, P))
                    v.tensor_tensor(m_w[:, 4 * n:4 * n + 4], misc_ps[n][:].rearrange("p (a b) -> p a b", a=4), u,
                                    ALU.add).then_inc(m_drained[n], 1)
                    dve.wait_ge(m_drained[n], m_count(n, i, F_R) + 1)
                v.tensor_scalar(m_w[:], m_w[:], 0.0, None, ALU.min).then_inc(w_sum, 1)

            def mask_chunk_weights(i):
                dve.wait_ge(w_exp, i + 1)
                v.tensor_tensor(m_w[:], m_w[:], notbefore[:].unsqueeze(1).to_broadcast((P, NC, P)), ALU.mult)\
                    .then_inc(w_mask, 1)

            def weighted_keys(i):
                for n in range(2):
                    dve.wait_ge(m_filled[n], m_count(n, i, F_MK) + 1)
                    w = h_tok[:, 3, 4 * n:4 * n + 4].unsqueeze(2).to_broadcast((P, 4, P))
                    v.tensor_tensor(m_ktok[:, 4 * n:4 * n + 4], misc_ps[n][:].rearrange("p (a b) -> p a b", a=4), w,
                                    ALU.mult).then_inc(m_drained[n], 1)

            def chunk_scores(i, cc):
                dve.wait_ge(m_filled[0], m_count(0, i, F_CHUNK + cc) + 1)
                if cc == 0:
                    dve.wait_ge(w_mask, i + 1)
                v.tensor_tensor(m_s[:], misc_ps[0][:, 0:P], m_w[:, cc], ALU.mult).then_inc(m_drained[0], 1)
                dve.wait_ge(m_filled[2], m_count(2, i, cc) + 1)
                dve.wait_ge(qc_done, i * NC + cc + 1)
                v.scalar_tensor_tensor(out=m_state[:], in0=m_state[:], scalar=h_dec[:, cc:cc + 1],
                                       in1=misc_ps[2][:, 0:P + 1], op0=ALU.mult, op1=ALU.add)\
                    .then_inc(m_drained[2], 1)

            def aggregate(cc):
                link.mark(v.bn_aggr(mv[:, cc], stat[:, cc]))

            def chunk_values(i, cc):
                dve.wait_ge(m_filled[1], m_count(1, i, F_CHUNK + cc) + 1)
                link(v.tensor_scalar(m_tmp[:], misc_ps[1][:, 0:P + 1], h_tok[:, 1, cc:cc + 1], None, ALU.mult))
                v.tensor_tensor(m_num[:, cc], misc_ps[1][:, 2 * P:3 * P + 1], m_tmp[:], ALU.add)\
                    .then_inc(m_drained[1], 1)
                if cc:
                    aggregate(cc - 1)
                dve.wait_ge(m_drained[1], m_count(1, i, F_CHUNK + cc) + 1)
                link.mark(v.bn_stats(stat[:, cc], m_num[:, cc, 0:P]))

            def newton(y, var, tmp):
                link(v.tensor_tensor(tmp, y, y, ALU.mult))
                link(v.scalar_tensor_tensor(out=tmp, in0=var, scalar=EPS, in1=tmp, op0=ALU.add, op1=ALU.mult))
                link(v.tensor_scalar(tmp, tmp, -0.5, 1.5, ALU.mult, ALU.add))
                link(v.tensor_tensor(y, y, tmp, ALU.mult))

            def norm_head(i):
                den, rden, var, y, tmp, rr = [small[:, 8 * n:8 * n + 8] for n in range(6)]
                link(v.tensor_copy(den, m_num[:, :, P]))
                link.mark(v.scalar_tensor_tensor(out=rden, in0=den, scalar=-1.0, in1=den, op0=ALU.mult, op1=ALU.max))
                aggregate(NC - 1)
                link.wait()
                link(v.tensor_tensor(den, rden, h_tok[:, 2, :], ALU.max))
                link(v.reciprocal(rden, den))
                link(v.tensor_tensor(tmp, rden, rden, ALU.mult))
                v.tensor_tensor(var, mv[:, :, 1], tmp, ALU.mult).then_inc(var_done, 1)
                dve.wait_ge(rstd_exp, i + 1)
                newton(y, var, tmp)
                link(v.tensor_tensor(rr, y, rden, ALU.mult))
                for cc in range(NC):
                    v.tensor_scalar(m_num[:, cc, 0:P], m_num[:, cc, 0:P], mv[:, cc, 0:1], rr[:, cc:cc + 1],
                                    ALU.subtract, ALU.mult).then_inc(hn_done, 1)

            def gate_head(i):
                for n in range(2):
                    dve.wait_ge(m_gate_done, i + 1)
                    dve.wait_ge(m_filled[n], m_count(n, i, F_HN) + 1)
                    v.scalar_tensor_tensor(out=m_w[:, 4 * n:4 * n + 4].rearrange("p a b -> p (a b)"),
                                           in0=misc_ps[n][:], scalar=h_col[:, H_NG:H_NG + 1],
                                           in1=m_gate[:, halves(n)], op0=ALU.mult, op1=ALU.mult)\
                        .then_inc(m_drained[n], 1)
                for n in range(2):
                    dve.wait_ge(m_drained[n], m_count(n, i, F_HN) + 1)

            def place0(i, s):
                if s == 4:
                    gate_y(i, 0)
                if s == 0:
                    conv_sum(i, 0)
                    conv_sum(i, 1)
                if s == 1:
                    conv_bound(i, 0)
                    pair_gate(i)
                if s == 2:
                    conv_silu(i, 0)
                    conv_sum(i, 2)
                    conv_sum(i, 3)
                if s == 3:
                    conv_bound(i, 1)
                    weighted_keys(i)
                if s >= 4:
                    chunk_scores(i, s - 4)

            def place1(i, s):
                if s == 0:
                    chunk_weights(i)
                if s == 1:
                    mask_chunk_weights(i)
                if s == 3:
                    conv_silu(i, 1)
                if s >= 4:
                    chunk_values(i, s - 4)

            def iteration(i, last):
                segs, end = segments(last)
                cap_sig(i * 2)
                head_columns(i, last)
                split_pair(i)
                tasks(i, -1, PRE, last)
                for s in range(NS):
                    p0, p1, p2, p3 = segs[s]
                    sum_zero(i, s)
                    tasks(i, p0, p1, last)
                    place0(i, s)
                    softplus(i, s)
                    softplus_low(i, s)
                    tasks(i, p1, p2, last)
                    place1(i, s)
                    mask_weights(i, s)
                    carry_high(i, s)
                    tasks(i, p2, p3, last)
                norm_head(i)
                tasks(i, segs[-1][3], end, last)
                gate_y(i, 1)
                gate_head(i)

            per = 56
            with dve.Fori(0, NH - 1) as i:
                link.enter(i, per)
                iteration(i, False)
            link.leave(NH - 1, "iteration")
            link.enter(0, 0)
            iteration(NH - 1, True)
            link.base, link.k = link.base + link.k, 0

            dve.sem_inc(yT_done, 1)

            def low_parts(r):
                for p in range(NH):
                    dve.wait_ge(yb_H, NH * r + p + 1)
                    v.tensor_tensor(ybL[r][:, p], yT[:, NH * r + p], ybH[r][:, p], ALU.subtract)\
                        .then_inc(yb_L, 1)

            def merge_tile(m, first, last):
                nth = lambda q: m * 6 + (END_CHUNKS + q + 1)
                for r in range(2):
                    for half in range(2):
                        dve.wait_ge(drained[half], m * 4 + (END_JOBS + r + 1))
                        q = 3 + 2 * r + half
                        if not first and not (last and q >= 6):
                            split_low((END_CHUNKS + q) % 3, nth(q))
                    z = (sigs, sigm)[r]
                    v.tensor_scalar(z[:], z[:], EXP_CAP, None, ALU.min).then_inc(g_capped[r], 1)
                    if first:
                        low_parts(r)
                        if r == 0:
                            split_low((END_CHUNKS + 6) % 3, nth(6))
                if last:
                    w_out_low(0, 4)
                row = lambda half: yT[:, bass.ds(m, 1), halves(half)].rearrange("p a s -> p (a s)")
                for half in range(2):
                    dve.wait_ge(filled[half], m * 4 + (END_JOBS + 3))
                    dve.wait_ge(g_done[0], m + 1)
                    if first and half == 0:
                        dve.wait_ge(yb_L, 2 * NH)
                    v.tensor_tensor(row(half), proj_ps[half][:], sigs[:, halves(half)], ALU.mult)\
                        .then_inc(drained[half], 1)
                    if last:
                        w_out_low(4 + 4 * half, 8 + 4 * half)
                if not last:
                    split_low((END_CHUNKS + 7) % 3, nth(7))
                for half in range(2):
                    dve.wait_ge(filled[half], m * 4 + (END_JOBS + 4))
                    dve.wait_ge(g_done[1], m + 1)
                    v.tensor_tensor(m_prod[:], proj_ps[half][:], sigm[:, halves(half)], ALU.mult)\
                        .then_inc(drained[half], 1)
                    dve.wait_ge(drained[half], m * 4 + (END_JOBS + 4))
                    v.tensor_tensor(row(half), row(half), m_prod[:], ALU.add).then_inc(yT_done, 1)
                    dve.wait_ge(yT_done, m * 2 + (half + 2))
                if last:
                    w_out_low(12, 16)
                else:
                    split_low((END_CHUNKS + 8) % 3, nth(8))

            def w_out_low(lo, hi):
                for n in range(lo, hi):
                    dve.wait_ge(woH_done, n + 1)
                    v.tensor_tensor(hL[:, n // 2, halves(n % 2)], raw[:, halves(n % 2)],
                                    hH[:, n // 2, halves(n % 2)], ALU.subtract).then_inc(woL_done, 1)

            def gate_sum(k):
                dve.wait_ge(raw_in, 16 * (k + 1))
                if k == 0:
                    v.tensor_scalar(g_acc[:], raw[:], silu_c[:, 0:1], None, ALU.mult).then_inc(g_acc_step, 1)
                else:
                    v.scalar_tensor_tensor(out=g_acc[:], in0=raw[:], scalar=silu_c[:, k:k + 1], in1=g_acc[:],
                                           op0=ALU.mult, op1=ALU.add).then_inc(g_acc_step, 1)
                dve.wait_ge(g_acc_step, k + 1)

            merge_tile(0, True, False)
            link.base, link.k = link.base + link.k, 0
            for k in range(KT):
                gate_sum(k)
            with dve.Fori(1, KT - 1) as m:
                link.enter(m - 1, 0)
                merge_tile(m, False, False)
            link.leave(KT - 2, "merge")
            link.enter(0, 0)
            merge_tile(KT - 1, False, True)
            link.base, link.k = link.base + link.k, 0

            dve.wait_ge(bc_in, 48)
            for n in range(2):
                dve.wait_ge(m_filled[n], m_count(n, NH, 0) + 1)
                h = halves(n)
                v.scalar_tensor_tensor(out=gate1[:, h], in0=misc_ps[n][:], scalar=1.0, in1=gate1[:, h],
                                       op0=ALU.add, op1=ALU.add).then_inc(gate_done, 1)

            def y_low(r, q):
                dve.wait_ge(yH_done, r * 2 + q + 1)
                v.tensor_tensor(yL[:, q], yT[:, :, bass.ds(r * 2 * P + q * P, P)], yH[:, q], ALU.subtract)\
                    .then_inc(yL_done, 1)

            y_low(0, 0)
            y_low(0, 1)
            dve.wait_ge(gate_done, 2)

            def norm_tile(r, q, first, last):
                row = res[:, q]
                if not first:
                    dve.wait_ge(stored[q], r * 16)
                for half in range(2):
                    dve.wait_ge(filled[half], r * 2 + (END_JOBS + 4 * KT + q + 1))
                    v.tensor_tensor(row[:, halves(half)], proj_ps[half][:], gate1[:, halves(half)], ALU.mult)\
                        .then_inc(drained[half], 1)
                for half in range(2):
                    dve.wait_ge(drained[half], r * 2 + (END_JOBS + 4 * KT + q + 1))
                dve.wait_ge(x_tile_in[q], r * 16 + 16)
                link(v.scalar_tensor_tensor(out=row, in0=x_in[:, q], scalar=ALPHA, in1=row, op0=ALU.mult,
                                            op1=ALU.add))
                for half in range(2):
                    v.bn_stats(stat_out[:, q, half], row[:, halves(half)]).then_inc(dve_step, 1)
                link.k += 2
                link.wait()
                if not last:
                    y_low(r + 1, q)
                c0 = 8 * q
                v.bn_aggr(small[:, c0:c0 + 2], stat_out[:, q].rearrange("p a b -> p (a b)")).then_inc(var_done, 1)
                dve.wait_ge(rstd_exp, r * 2 + (NH + q + 1))
                newton(small[:, c0 + 2:c0 + 3], small[:, c0 + 1:c0 + 2], small[:, c0 + 3:c0 + 4])
                link(v.tensor_scalar(row, row, small[:, c0:c0 + 1], small[:, c0 + 2:c0 + 3], ALU.subtract, ALU.mult))
                link(v.tensor_tensor(row, row, lng[:], ALU.mult))
                v.tensor_tensor(row, row, lnb[:], ALU.add).then_inc(out_done, 1)

            def out_pair(r, first, last):
                for q in range(2):
                    norm_tile(r, q, first, last)

            out_pair(0, True, False)
            link.base, link.k = link.base + link.k, 0
            with dve.Fori(1, NC // 2 - 1) as r:
                link.enter(r - 1, 18)
                out_pair(r, False, False)
            link.leave(NC // 2 - 2, "output")
            out_pair(NC // 2 - 1, False, True)


_INS = ["x", "c", "w_ada", "b_ada", "w_in", "b_in", "conv_w", "conv_b", "ml_norm_g", "w_sb_proj", "w_ml_proj",
        "w_out", "ln_g", "ln_b"]


def kernel(**inputs):
    import numpy as _np
    import concourse.bacc as _bacc
    from concourse.bass_utils import run_bass_kernel_spmd as _run

    nc = _bacc.Bacc("TRN2", target_bir_lowering=False, num_devices=1)
    arrays, args = {}, []
    for name in _INS:
        a = _np.ascontiguousarray(inputs[name])
        arrays[f"in_{name}"] = a
        args.append(nc.dram_tensor(f"in_{name}", a.shape, mybir.dt.from_np(a.dtype), kind="ExternalInput").ap())
    out = nc.dram_tensor("out_y", (1, S, D), F32, kind="ExternalOutput").ap()
    build_kernel(nc, *args, out)
    r = _run(nc, [arrays], core_ids=[0])
    return r.results[0]["out_y"]
```

```python
from contextlib import ExitStack

import concourse.bass as bass
from concourse import mybir

ALU = mybir.AluOpType
ACT = mybir.ActivationFunctionType
F32 = mybir.dt.float32
F32R = mybir.dt.float32r

P = 128
D = 1024
S = 1024
KT = D // P
HALF = 512
W_SB = 512
W_ML = 512
NH = W_ML // P
NC = S // P
SB_SCALE = 64 ** -0.5
ML_SCALE = 128 ** -0.5
ALPHA = 2.0 ** 0.25
EPS = 1e-5
SOFT_CAP = 30.0
EXP_CAP = 2.0 ** 62

OFF_SB = [0, W_SB, 2 * W_SB, 3 * W_SB]
OFF_ML = [4 * W_SB + n * W_ML for n in range(5)]
OFF_IF = 4 * W_SB + 5 * W_ML
OFF_GSB = OFF_IF + 2 * NH
OFF_GML = OFF_GSB + D

ROW_B = 0
ROW_GSB = 36
ROW_GML = 44
ROW_CW = 52
ROW_CB = 84
ROW_NG = 92
ROW_ADA = 96
ROW_C = 120

JOB_MM = 3 * KT * 2
PRO_JOBS = 5
JOBS = ["mlk", "mlq", "mlv", "mlo", "mlz", "sbq", "sbk", "sbv", "sbz"]
JOBS_LAST = JOBS[:5] + ["gml0", "gsb0", "gsb1", "gsb2"]
NJ = len(JOBS)
GATE_0 = 3
J_GATES = PRO_JOBS + NH * NJ
J_MERGE = J_GATES + KT - GATE_0
J_OUT = J_MERGE + 3 * KT - 1
C_GATES, C_MERGE = 2 * J_GATES, 2 * J_MERGE


def merge_job(m, r):
    return m * 3 + (J_MERGE - 1 + r)


def merge_chunk(m, q):
    return m * 4 + (C_MERGE - 2 + q)


def merge_slot(u, q):
    return (u * 4 + (C_MERGE - 2 + q)) % 3

SLOTS = [(tc, j) for tc in range(2) for j in range(4 * tc + 3, -1, -1)]
NS = len(SLOTS)


def first_col(s):
    tc, j = SLOTS[s]
    return max(0, P * (j - 4 * tc))


def diagonal(s):
    tc, j = SLOTS[s]
    return j >= 4 * tc


def opens(s):
    tc, j = SLOTS[s]
    return j == 4 * tc + 3


def closes(s):
    return SLOTS[s][1] == 0


def diagonals(s):
    return sum(diagonal(x) for x in range(s))


def carries(s):
    return sum(not closes(x) for x in range(s))


ND, NCAR = diagonals(NS), carries(NS)
PRE = 48
ADA_FIRST = 3


def segments():
    at, out = PRE, []
    for s in range(NS):
        sizes = (10, 10, 12) if s < 3 else (10, 10, 10)
        row = [at]
        for n in sizes:
            at += n
            row.append(at)
        out.append(row)
    return out, JOB_MM * NJ


def events(lo, hi):
    n = NJ
    found = [(JOB_MM * 4 + 6, 2, "o_log", 0, 0), (JOB_MM * 5 + 6, 2, "z_log", 0, 0),
             (JOB_MM * 5 + 14, 2, "z_exp", 0, 0), (JOB_MM * 5 + 22, 2, "z_mul", 0, 0)]
    for j in range(n):
        found += [(JOB_MM * j + 24, 0, "evac", j, 0), (JOB_MM * (j + 1), 0, "evac", j, 1)]
    for c in range(2, 2 * n + 2):
        j, odd = divmod(c - 3, 2)
        found.append((JOB_MM * j + 36 + 12 * odd, 1, "split", c, 0))
    return [e[2:] for e in sorted(found) if lo < e[0] <= hi]


class Chain:

    def __init__(self, eng, semaphore):
        self.eng, self.semaphore, self.base, self.k, self.i, self.per = eng, semaphore, 0, 0, 0, 0

    def enter(self, i, per):
        self.i, self.per, self.k = i, per, 0

    def leave(self, rounds, where):
        assert self.k == self.per, (where, self.k, self.per)
        self.base, self.k, self.i, self.per = self.base + rounds * self.per, 0, 0, 0

    def mark(self, instruction):
        self.k += 1
        instruction.then_inc(self.semaphore, 1)

    def wait(self):
        self.eng.wait_ge(self.semaphore, self.i * self.per + (self.base + self.k))

    def __call__(self, instruction):
        self.mark(instruction)
        self.wait()


def build_kernel(nc, x, c, w_ada, b_ada, w_in, b_in, conv_w, conv_b, ml_norm_g, w_sb_proj, w_ml_proj, w_out,
                 ln_g, ln_b, out):
    ysb_dram = nc.dram_tensor("ysb_scratch", (NH, P, S), F32, kind="Internal").ap()
    yml_dram = nc.dram_tensor("yml_scratch", (NH, P, S), F32, kind="Internal").ap()
    w_in_v = w_in[0].rearrange("(k p) c -> p k c", p=P)
    w_ada_v = w_ada[0].rearrange("(k p) c -> p k c", p=P)
    w_sbp_v = w_sb_proj[0].rearrange("(k p) c -> p k c", p=P)
    w_mlp_v = w_ml_proj[0].rearrange("(k p) c -> p k c", p=P)
    w_out_v = w_out[0].rearrange("(k p) c -> p k c", p=P)
    x_v = x[0].rearrange("(t p) d -> p t d", p=P)
    out_v = out[0].rearrange("(t p) d -> p t d", p=P)

    with ExitStack() as ctx:
        def sb(name, shape, dt=F32, to=None):
            return (to or ctx).enter_context(nc.sbuf_tensor(name, shape, dt))

        def sem(name):
            return ctx.enter_context(nc.semaphore(name))

        bank = [ctx.enter_context(nc.psum_tensor(f"bank{n}", [P, HALF], F32)) for n in range(8)]
        proj_ps, z_ps, y_ps, misc_ps = bank[0:2], bank[2:4], bank[4], bank[5:8]

        hH = sb("hH", [P, KT, S], F32R)
        hL = sb("hL", [P, KT, S], F32R)
        w_raw = sb("w_raw", [P, 3, 4, P])
        wH = sb("wH", [P, 3, 4, P], F32R)
        wL = sb("wL", [P, 3, 4, P], F32R)
        cols = sb("cols", [P, P])
        ncols = sb("ncols", [P, P])
        silu_c = sb("silu_c", [P, KT])
        r_bias = sb("r_bias", [P, 1])
        ident = sb("ident", [P, P])
        ones = sb("ones", [P, P])
        stat_out = sb("stat_out", [P, 2, 2, 6])
        small = sb("small", [P, 48])

        loop = ExitStack()
        lt = lambda name, shape, dt=F32: sb(name, shape, dt, loop)
        next_q, next_k = lt("next_q", [P, S]), lt("next_k", [P, S])
        next_v, next_g = lt("next_v", [P, S]), lt("next_g", [P, S])
        later = lt("later", [P, P])
        notbefore = lt("notbefore", [P, P])
        neg_upto = lt("neg_upto", [P, P], F32R)
        neg_ones = lt("neg_ones", [P, P], F32R)
        sel_all = lt("sel_all", [P, NH, P])
        tok = lt("tok", [P, NC, 4, NH])
        dec = lt("dec", [P, NC, NH])
        bm = lt("bm", [P, S])
        sig = lt("sig", [P, S])
        inner = ExitStack()
        it = lambda name, shape, dt=F32: sb(name, shape, dt, inner)
        qH, qL = it("qH", [P, S], F32R), it("qL", [P, S], F32R)
        kH, kL = it("kH", [P, S], F32R), it("kL", [P, S], F32R)
        v_tok = it("v_tok", [P, NC, P])
        g_cur = it("g_cur", [P, S])
        soft = [it(f"soft{h}", [P, HALF]) for h in range(2)]
        spH = [it(f"spH{h}", [P, HALF], F32R) for h in range(2)]
        spL = [it(f"spL{h}", [P, HALF], F32R) for h in range(2)]
        tsum = [it(f"tsum{h}", [P, HALF]) for h in range(2)]
        tsH = [it(f"tsH{h}", [P, HALF], F32R) for h in range(2)]
        tsL = [it(f"tsL{h}", [P, HALF], F32R) for h in range(2)]
        y_stage = it("y_stage", [P, HALF])
        conv_in = it("conv_in", [P, 4 + S])
        m_q, m_k = it("m_q", [P, S]), it("m_k", [P, S])
        m_vraw = it("m_vraw", [P, S])
        m_gate = it("m_gate", [P, S])
        m_ktok = it("m_ktok", [P, NC, P])
        m_vtok = it("m_vtok", [P, NC, P + 1])
        m_num = it("m_num", [P, NC, P + 1])
        m_w = it("m_w", [P, NC, P])
        m_state = it("m_state", [P, P + 1])
        m_s = it("m_s", [P, P])
        m_tmp = it("m_tmp", [P, P + 1])
        h_tok = it("h_tok", [P, 4, NC])
        h_dec = it("h_dec", [P, NC])
        h_col = it("h_col", [P, 56])
        sel_cur = it("sel_cur", [P, P])
        stat = it("stat", [P, NC, 6])
        mv = it("mv", [P, NC, 2])
        inner.close()
        pro = ExitStack()
        pt = lambda name, shape, dt=F32: sb(name, shape, dt, pro)
        x_rows = pt("x_rows", [P, NC, D])
        a_raw = pt("a_raw", [P, 4, D])
        a_acc = pt("a_acc", [P, 2, D])
        upto = pt("upto", [P, P])
        prm = pt("prm", [P, P])
        mod = pt("mod", [P, 2, KT])
        xT = pt("xT", [P, KT, S])
        pro.close()
        rows_ctx = ExitStack()
        rt = lambda name, shape, dt=F32: sb(name, shape, dt, rows_ctx)
        r_i, r_f, r_e = rt("r_i", [P, S]), rt("r_f", [P, S]), rt("r_e", [P, S])
        r_b, r_m, r_q = rt("r_b", [P, S]), rt("r_m", [P, S]), rt("r_q", [P, S])
        r_one = rt("r_one", [P, S])
        r_if = rt("r_if", [P, S])
        rows_ctx.close()
        loop.close()
        after = ExitStack()
        at = lambda name, shape, dt=F32: sb(name, shape, dt, after)
        sigm = at("sigm", [P, S])
        yT = at("yT", [P, KT, S])
        m_prod = at("m_prod", [P, HALF])
        raw = at("raw", [P, 2, D])
        g_acc = at("g_acc", [P, D])
        merge = ExitStack()
        mt = lambda name, shape, dt=F32: sb(name, shape, dt, merge)
        ybH = [mt("ysbH", [P, NH, S], F32R), mt("ymlH", [P, NH, S], F32R)]
        ybL = [mt("ysbL", [P, NH, S], F32R), mt("ymlL", [P, NH, S], F32R)]
        stage = mt("stage", [P, 2, S])
        merge.close()
        yH = at("yH", [P, 2, KT, P], F32R)
        yL = at("yL", [P, 2, KT, P], F32R)
        x_in = at("x_in", [P, 2, D])
        res = at("res", [P, 2, D])
        gate1, lng, lnb = at("gate1", [P, D]), at("lng", [P, D]), at("lnb", [P, D])
        after.close()

        params_in, x_rows_in, bias_in = sem("params_in"), sem("x_rows_in"), sem("bias_in")
        a_in = [sem(f"ada_in{n}") for n in range(4)]
        w_in_s = [sem(f"weights_in{n}") for n in range(3)]
        consts, consts_r = sem("consts_made"), sem("consts_rounded")
        cols_done, c_exp, silu_done = sem("cols_done"), sem("c_exp"), sem("silu_done")
        ada_used, ada_done, mod_done = sem("ada_used"), sem("ada_done"), sem("mod_done")
        h_full, hH_done, hL_done = sem("h_full"), sem("hH_done"), sem("hL_done")
        rows_zero, rows_in, f_ln = sem("rows_zero"), sem("rows_in"), sem("f_ln")
        q_rows, q_exp, tok_done = sem("q_rows"), sem("q_exp"), sem("tok_done")
        wH_done, wL_done = sem("wH_done"), sem("wL_done")
        w_first_used = sem("w_first_used")
        filled = [sem(f"proj_filled{h}") for h in range(2)]
        drained = [sem(f"proj_drained{h}") for h in range(2)]
        m_filled = [sem(f"misc_filled{n}") for n in range(3)]
        m_drained = [sem(f"misc_drained{n}") for n in range(3)]
        sig_exp, sig_capped, sig_log, sig_done = sem("sig_exp"), sem("sig_capped"), sem("sig_log"), sem("sig_done")
        sig_used, g_made = sem("sig_used"), sem("g_made")
        o_capped, o_log, z_sum, m_gate_done = sem("o_capped"), sem("o_log"), sem("z_sum"), sem("m_gate_done")
        two = lambda name: [sem(f"{name}{h}") for h in range(2)]
        z_done, ex_done, ln_done = two("z_done"), two("ex_done"), two("ln_done")
        sp_raw, sp_done, spH_done, spL_done = two("sp_raw"), two("sp_done"), two("spH_done"), two("spL_done")
        ts_zero, ts_sum, tsH_done, tsL_done = two("ts_zero"), two("ts_sum"), two("tsH_done"), two("tsL_done")
        e_done, a_exp, a_mask, pv_done = two("e_done"), two("a_exp"), two("a_mask"), two("pv_done")
        y_staged, y_stored = sem("y_staged"), sem("y_stored")
        pair_split, h_cols = sem("pair_split"), sem("h_cols_done")
        conv_acc, conv_done, conv_pad = sem("conv_acc"), sem("conv_done"), sem("conv_pad")
        conv_exp, conv_cap, conv_log, conv_sig = sem("conv_exp"), sem("conv_cap"), sem("conv_log"), sem("conv_sig")
        w_sum, w_exp, w_mask = sem("w_sum"), sem("w_exp"), sem("w_mask")
        state_zero, qc_done = sem("state_zero"), sem("qc_done")
        var_done, rstd_ln, rstd_exp = sem("var_done"), sem("rstd_ln"), sem("rstd_exp")
        hn_done, yml_stored = sem("hn_done"), sem("yml_stored")
        dve_step = sem("dve_step")
        y_in, yb_H, yb_L = [sem("y_in0"), sem("y_in1")], sem("yb_H"), sem("yb_L")
        raw_in, g_acc_step = [sem("gate_rows_in0"), sem("gate_rows_in1")], sem("g_acc_step")
        wo_in = [sem(f"w_out_in{n}") for n in range(7)]
        free = sem("loop_over")
        woH_done, woL_done = sem("woH_done"), sem("woL_done")
        g_capped, g_log, g_done = sem("gate_capped"), sem("gate_log"), sem("gate_sigmoid")
        yT_done, yH_done, yL_done, bc_in = sem("yT_done"), sem("yH_done"), sem("yL_done"), sem("broadcast_in")
        x_tile_in = [sem("x_tile_in0"), sem("x_tile_in1")]
        stored = [sem("stored0"), sem("stored1")]
        out_done, gate_done = sem("out_done"), sem("gate_done")
        nbias_done, normed = sem("mean_rstd_done"), sem("normed")

        block = ctx.enter_context(nc.Block())

        M_PRO, M_PER = [10, 9, 1], [13, 13, 8]
        F_V, F_R, F_MK, F_MV, F_CHUNK, F_HN = 0, 1, 2, 3, 4, 12

        def m_count(n, i, k):
            return i * M_PER[n] + (M_PRO[n] + k)

        def job(i, j):
            return i * NJ + (PRO_JOBS + j)

        def chunk(i, c_):
            return i * 2 * NJ + (2 * PRO_JOBS + c_)

        def gate_buffer(n):
            return sigm if n == 0 or n > KT else yT[:, n - 1]

        wo_buffer = [raw[:, n // 2, (n % 2) * HALF:(n % 2 + 1) * HALF] for n in range(4)] + [
            w_raw[:, merge_slot(KT - 1, q)].rearrange("p k c -> p (k c)") for q in (1, 2, 3)]

        def conv_buffer(k):
            return (m_num[:, :, 0:P], sig[:].rearrange("p (c t) -> p c t", t=P))[k]

        def halves(h):
            return slice(h * HALF, (h + 1) * HALF)

        GROUP = {"sbq": 0, "sbk": 1, "sbv": 2, "sbz": 3, "mlq": 4, "mlk": 5, "mlv": 6, "mlo": 7, "mlz": 8}
        H_NEXT, H_TAP, H_CB, H_NG, H_NEG = 9, {"q": 18, "k": 22}, {"q": 26, "k": 27}, 28, 32

        def bias_of(name, negative=False):
            n = GROUP[name] + (H_NEXT if name[:2] == "sb" else 0) + (H_NEG if negative else 0)
            return h_col[:, n:n + 1]

        @block.sync
        def _(sp):
            bi = b_in[0]
            rows = [
                (ROW_C, c[0]), (ROW_ADA, b_ada[0]), (ROW_B, bi[0:OFF_IF]),
                (ROW_GSB, bi[OFF_GSB:OFF_GSB + 2 * D]), (ROW_CB, conv_b[0]), (ROW_NG, ml_norm_g[0]),
            ]
            for row, src in rows:
                src = src.rearrange("(t p) -> t p", p=P)
                sp.dma_start(prm[row:row + src.shape[0], :], src).then_inc(params_in, 16)
            sp.dma_start(prm[ROW_CW:ROW_CW + 4 * KT, :], conv_w[0].rearrange("j (t p) -> (j t) p", p=P))\
                .then_inc(params_in, 16)

            for t in range(NC):
                sp.dma_start(x_rows[:, t], x_v[:, t]).then_inc(x_rows_in, 16)

            def load(slot, src, split):
                if split is not None:
                    sp.wait_ge(wL_done, split)
                sp.dma_start(w_raw[:, slot, :, 0:src.shape[2]], src).then_inc(w_in_s[slot], 16)

            def pro_load(g):
                n, q = divmod(g, 2)
                off, width = ([(OFF_IF, 2 * NH)] + [(o, P) for o in OFF_SB])[n]
                load(g % 3, w_in_v[:, 4 * q:4 * q + 4, off:off + width], g - 2 if g >= 3 else None)

            for g in range(3):
                pro_load(g)
            for n in range(2 * KT):
                k, what = divmod(n, 2)
                if n >= 4:
                    sp.wait_ge(ada_used, n - 3)
                sp.dma_start(a_raw[:, n % 4], w_ada_v[:, k, what * D:(what + 1) * D]).then_inc(a_in[n % 4], 16)
            for g in range(3, 2 * PRO_JOBS):
                pro_load(g)

            off = dict(zip(("mlq", "mlk", "mlv", "mlo", "mlz"), OFF_ML)) |\
                dict(zip(("sbq", "sbk", "sbv", "sbz"), [o + P for o in OFF_SB]))

            def iteration(i, last):
                fixed = (lambda v: v) if last else sp.snap
                for j, name in enumerate(JOBS_LAST if last else JOBS):
                    start = fixed(i * P + off[name]) if name in off else \
                        {"gsb": OFF_GSB, "gml": OFF_GML}[name[:3]] + int(name[3]) * P
                    for q in range(2):
                        slot, split = (2 * PRO_JOBS + 2 * j + q) % 3, fixed(chunk(i, 2 * j + q) - 2)
                        load(slot, w_in_v[:, 4 * q:4 * q + 4, bass.ds(start, P)], split)

            with sp.Fori(0, NH - 1) as i:
                iteration(i, False)
            iteration(NH - 1, True)

            for m in range(GATE_0, KT):
                for q in range(2):
                    g = C_GATES + 2 * (m - GATE_0) + q
                    load(g % 3, w_in_v[:, 4 * q:4 * q + 4, OFF_GSB + m * P:OFF_GSB + (m + 1) * P], g - 2)

            def merge_loads(m, u, first):
                fixed = (lambda z: z) if isinstance(m, int) else sp.snap
                start = [fixed(m * P + OFF_GML), fixed(m * P)]
                for q, (src, n) in enumerate([(w_in_v[:, 0:4], 0), (w_in_v[:, 4:8], 0), (w_sbp_v, 1), (w_mlp_v, 1)]):
                    if first and q < 2:
                        continue
                    split = None if q == 2 and not first else fixed(merge_chunk(m, q) + ((q == 1) - 2))
                    load(merge_slot(u, q), src[:, :, bass.ds(start[n], P)], split)

            merge_loads(0, 0, True)
            with sp.Fori(0, (KT - 2) // 3) as g:
                for u in range(3):
                    merge_loads(g * 3 + (u + 1), u + 1, False)
            merge_loads(KT - 1, KT - 1, False)
            for n in range(2 * KT):
                if n < 4:
                    sp.wait_ge(g_acc_step, KT)
                elif n < 7:
                    sp.wait_ge(wL_done, merge_chunk(KT - 1, n - 3) + 1)
                else:
                    sp.wait_ge(woL_done, n - 6)
                sp.dma_start(wo_buffer[n % 7], w_out_v[:, n // 2, halves(n % 2)]).then_inc(wo_in[n % 7], 16)

            sp.wait_ge(filled[1], J_OUT)
            sp.dma_start(gate1[:], b_ada[0:1, 2 * D:3 * D].broadcast_to((P, D))).then_inc(bc_in, 16)
            sp.dma_start(lng[:], ln_g[0:1, :].broadcast_to((P, D))).then_inc(bc_in, 16)
            sp.dma_start(lnb[:], ln_b[0:1, :].broadcast_to((P, D))).then_inc(bc_in, 16)
            for q in range(2):
                sp.dma_start(x_in[:, q:q + 1], x_v[:, q:q + 1]).then_inc(x_tile_in[q], 16)

            def pair(r, last):
                fixed = (lambda v: v) if last else sp.snap
                at_ = [fixed(r * 2 + q) for q in range(4)]
                done = [fixed(r * 2 + q + 1) for q in range(2)]
                for q in range(2):
                    sp.wait_ge(out_done, done[q])
                    sp.dma_start(out_v[:, bass.ds(at_[q], 1)], res[:, q:q + 1]).then_inc(stored[q], 16)
                    if not last:
                        sp.dma_start(x_in[:, q:q + 1], x_v[:, bass.ds(at_[2 + q], 1)]).then_inc(x_tile_in[q], 16)

            with sp.Fori(0, NC // 2 - 1) as r:
                pair(r, False)
            pair(NC // 2 - 1, True)
            for q in range(2):
                sp.wait_ge(stored[q], 16 * (NC // 2))

        @block.gpsimd
        def _(pool):
            g = nc.gpsimd
            g.memset(ident[:], 0.0).then_inc(consts, 1)
            g.memset(ones[:], 1.0).then_inc(consts, 1)
            g.memset(sel_all[:], 0.0).then_inc(consts, 1)
            g.memset(upto[:], -1.0).then_inc(consts, 1)
            pool.wait_ge(consts, 4)
            g.affine_select(out=ident[:], in_=ident[:], compare_op=ALU.not_equal, fill=1.0, base=0,
                            pattern=[[-1, P]], channel_multiplier=1).then_inc(consts, 1)
            g.affine_select(out=later[:], in_=ones[:], compare_op=ALU.is_gt, fill=0.0, base=0,
                            pattern=[[1, P]], channel_multiplier=-1).then_inc(consts, 1)
            g.affine_select(out=notbefore[:], in_=ones[:], compare_op=ALU.is_ge, fill=0.0, base=0,
                            pattern=[[1, P]], channel_multiplier=-1).then_inc(consts, 1)
            g.affine_select(out=upto[:], in_=upto[:], compare_op=ALU.is_ge, fill=0.0, base=0,
                            pattern=[[-1, P]], channel_multiplier=1).then_inc(consts, 1)
            g.affine_select(out=sel_all[:], in_=sel_all[:], compare_op=ALU.not_equal, fill=1.0, base=0,
                            pattern=[[-1, NH], [0, P]], channel_multiplier=1).then_inc(consts, 1)
            pool.wait_ge(consts, 9)
            g.affine_select(out=sel_all[:], in_=sel_all[:], compare_op=ALU.not_equal, fill=1.0, base=-32,
                            pattern=[[-1, NH], [0, P]], channel_multiplier=1).then_inc(consts, 1)
            pool.dma_start(r_bias[0:2 * NH, :], b_in[0, OFF_IF:OFF_GSB].rearrange("(p a) -> p a", a=1))\
                .then_inc(bias_in, 16)

            pool.wait_ge(m_filled[0], KT + 1)
            pool.wait_ge(m_filled[1], KT)
            for z in (r_i, r_f, r_if):
                g.memset(z[:], 0.0).then_inc(rows_zero, 1)
            g.memset(r_one[:], 1.0).then_inc(rows_zero, 1)
            pool.wait_ge(rows_zero, 4)
            g.memset(r_one[:, 0:S:P], 0.0).then_inc(rows_zero, 1)

            pool.wait_ge(drained[1], 1)
            for q in range(4):
                pool.dma_start(r_f[32 * q:32 * q + NH, :], r_if[NH:2 * NH, :]).then_inc(rows_in, 16)
                pool.dma_start(r_i[32 * q:32 * q + NH, :], r_if[0:NH, :]).then_inc(rows_in, 16)

            def carry_sums(i, s):
                if closes(s):
                    return
                f = first_col(s)
                for h in range(2):
                    pool.wait_ge(sp_done[h], i * NS + s + 1)
                    if opens(s):
                        pool.wait_ge(ts_zero[h], i * 2 + SLOTS[s][0] + 1)
                    else:
                        pool.wait_ge(tsL_done[h], i * NCAR + carries(s))
                    g.tensor_tensor(tsum[h][:, f:], tsum[h][:, f:], soft[h][:, f:], ALU.add).then_inc(ts_sum[h], 1)
                for h in range(2):
                    pool.wait_ge(tsH_done[h], i * NCAR + carries(s) + 1)
                    g.tensor_tensor(tsL[h][:, f:], tsum[h][:, f:], tsH[h][:, f:], ALU.subtract)\
                        .then_inc(tsL_done[h], 1)

            with pool.Fori(0, NH - 1) as i:
                for s in range(NS):
                    carry_sums(i, s)
            for s in range(NS):
                carry_sums(NH - 1, s)

            pool.wait_ge(free, 1)
            pool.wait_ge(y_stored, 16 * (2 * NH + 1))
            pool.wait_ge(yml_stored, 16 * (NH + 1))
            def load_y(n):
                if n >= 2:
                    pool.wait_ge(yb_L, n - 1)
                pool.dma_start(stage[:, n % 2], (ysb_dram if n < NH else yml_dram)[n % NH]).then_inc(y_in[n % 2], 16)

            def load_gate_rows(k):
                if k >= 2:
                    pool.wait_ge(g_acc_step, k - 1)
                pool.dma_start(raw[:, k % 2], w_ada_v[:, k, 2 * D:3 * D]).then_inc(raw_in[k % 2], 16)

            for n in range(NH):
                load_y(2 * n)
                load_y(2 * n + 1)
                load_gate_rows(2 * n)
                load_gate_rows(2 * n + 1)
            with pool.Fori(1, NC // 2) as r:
                for q in range(2):
                    pool.wait_ge(yH_done, r * 2 + q + 1)
                    g.tensor_tensor(yL[:, q], yT[:, :, bass.ds(r * 2 * P + q * P, P)], yH[:, q], ALU.subtract)\
                        .then_inc(yL_done, 1)

        @block.tensor
        def _(pe):
            t = nc.tensor

            def split_product(ps, lhs, rhs, k, kt, done=None):
                (aH, aL), (bH, bL) = lhs, rhs
                t.matmul(ps, aH, bH, start=k == 0, stop=False)
                t.matmul(ps, aH, bL, start=False, stop=False)
                return t.matmul(ps, aL, bH, start=False, stop=k == kt - 1)

            def project(i, lo, hi, base_job=None):
                for n in range(lo, hi):
                    j, r = divmod(n, JOB_MM)
                    half, r = divmod(r, JOB_MM // 2)
                    k, term = divmod(r, 3)
                    number = job(i, j) if base_job is None else base_job + j
                    first = chunk(i, 2 * j) if base_job is None else 2 * (base_job + j)
                    slot0 = (2 * PRO_JOBS + 2 * j if base_job is None else first) % 3
                    if half == 0 and term == 0 and k % 4 == 0:
                        pe.wait_ge(wL_done, first + (k // 4 + 1))
                    if r == 0:
                        pe.wait_ge(drained[half], number)
                    slot = (slot0 + k // 4) % 3
                    w = (wL if term == 2 else wH)[:, slot, k % 4]
                    a = (hL if term == 1 else hH)[:, k, halves(half)]
                    ins = t.matmul(proj_ps[half][:], w, a, start=(r == 0), stop=(r == JOB_MM // 2 - 1))
                    if r == JOB_MM // 2 - 1:
                        ins.then_inc(filled[half], 1)
                    elif half == 1 and r == 11:
                        ins.then_inc(w_first_used, 1)

            pe.wait_ge(consts, 5)
            pe.wait_ge(params_in, 16 * 7)
            t.transpose(misc_ps[0][:, 0:P], prm[:], ident[:]).then_inc(m_filled[0], 1)
            for f in range(2 * KT):
                half, d = divmod(f, KT)
                n = f % 2
                if d == 0:
                    pe.wait_ge(x_rows_in, 16 * NC)
                if f // 2 + (1 - n) > 0:
                    pe.wait_ge(m_drained[n], f // 2 + (1 - n))
                for q in range(4):
                    ins = t.transpose(misc_ps[n][:, q * P:(q + 1) * P], x_rows[:, 4 * half + q, d * P:(d + 1) * P],
                                      ident[:])
                ins.then_inc(m_filled[n], 1)
            for d in range(KT):
                if d == 0:
                    pe.wait_ge(ada_used, 2 * KT)
                for what in range(2):
                    col = what * KT + d
                    ins = t.matmul(z_ps[d >= ADA_FIRST][:, col:col + 1], a_acc[:, what, d * P:(d + 1) * P],
                                   ones[:, 0:1], start=True, stop=True)
                if d + 1 in (ADA_FIRST, KT):
                    ins.then_inc(ada_done, 1)

            def gate_columns():
                pe.wait_ge(q_exp, 3)
                for n in range(2):
                    pe.wait_ge(m_drained[n], M_PRO[n] - 1)
                    for q in range(4):
                        cc = 4 * n + q
                        ins = t.transpose(misc_ps[n][:, q * P:(q + 1) * P], r_q[:, cc * P:(cc + 1) * P], ident[:])
                    ins.then_inc(m_filled[n], 1)
                for h in range(NH):
                    ins = t.matmul(misc_ps[2][:, h * NC:(h + 1) * NC], sel_all[32:64, h, :],
                                   r_q[32:64, P - 1:S:P], start=True, stop=True)
                ins.then_inc(m_filled[2], 1)

            for k in range(KT):
                pe.wait_ge(hL_done, k + 1)
                for n in range(2):
                    if k % 4 == 0:
                        pe.wait_ge(wL_done, 2 * n + k // 4 + 1)
                    width = P if n else 2 * NH
                    slot = (2 * n + k // 4) % 3
                    for half in range(2):
                        ps = (proj_ps if n else misc_ps)[half][0:width, :]
                        ins = split_product(ps, (wH[:, slot, k % 4, 0:width], wL[:, slot, k % 4, 0:width]),
                                            (hH[:, k, halves(half)], hL[:, k, halves(half)]), k, KT)
                        if k == KT - 1:
                            ins.then_inc(filled[half], 1)
                        elif half == 1 and k == 3:
                            ins.then_inc(w_first_used, 1)
            for n in range(2, PRO_JOBS):
                project(0, 0, JOB_MM, base_job=n)
            gate_columns()

            def transposes(bank_no, srcs):
                for q, src in enumerate(srcs):
                    ins = t.transpose(misc_ps[bank_no][:, q * P:(q + 1) * P], src, ident[:])
                ins.then_inc(m_filled[bank_no], 1)

            def scores(i, s):
                tc, j = SLOTS[s]
                f = first_col(s)
                for h in range(2):
                    r = slice(64 * h, 64 * h + 64)
                    if s > 0:
                        pe.wait_ge(a_exp[h], i * NS + s)
                    elif h == 0:
                        pe.wait_ge(pair_split, i * 4 + 4)
                    q = slice(tc * HALF + f, (tc + 1) * HALF)
                    kk = slice(j * P, (j + 1) * P)
                    ps = z_ps[h][:, f:]
                    t.matmul(ps, kH[r, kk], qH[r, q], start=True, stop=False)
                    t.matmul(ps, kH[r, kk], qL[r, q], start=False, stop=False)
                    t.matmul(ps, kL[r, kk], qH[r, q], start=False, stop=True).then_inc(z_done[h], 1)

            def exponents(i, s):
                f = first_col(s)
                for h in range(2):
                    if not opens(s):
                        fp = first_col(s - 1)
                        pe.wait_ge(sp_done[h], i * NS + s + 1)
                        pe.wait_ge(tsL_done[h], i * NCAR + carries(s))
                        t.matmul(z_ps[h][:, fp:], neg_ones[:], tsH[h][:, fp:], start=False, stop=False,
                                 skip_group_check=True)
                        t.matmul(z_ps[h][:, fp:], neg_ones[:], tsL[h][:, fp:], start=False, stop=False,
                                 skip_group_check=True)
                    pe.wait_ge(spL_done[h], i * NS + s + 1)
                    t.matmul(z_ps[h][:, f:], neg_upto[:], spH[h][:, f:], start=False, stop=False,
                             skip_group_check=True)
                    t.matmul(z_ps[h][:, f:], neg_upto[:], spL[h][:, f:], start=False, stop=True,
                             skip_group_check=True).then_inc(e_done[h], 1)

            def weighted_values(i, s):
                tc, j = SLOTS[s]
                f = first_col(s)
                if s == 4:
                    pe.wait_ge(y_staged, i * 2 + 1)
                for h in range(2):
                    if diagonal(s):
                        pe.wait_ge(a_mask[h], i * ND + diagonals(s) + 1)
                    else:
                        pe.wait_ge(a_exp[h], i * NS + s + 1)
                    t.matmul(y_ps[64 * h:64 * h + 64, f:], v_tok[:, j, 64 * h:64 * h + 64], soft[h][:, f:],
                             start=opens(s), stop=closes(s), skip_group_check=True).then_inc(pv_done[h], 1)

            def mlstm_first(i, s):
                if s == 3:
                    for n in range(2):
                        pe.wait_ge(m_drained[n], m_count(n, i, F_MV))
                        if n == 0:
                            pe.wait_ge(drained[1], job(i, 2) + 1)
                        transposes(n, [m_vraw[:, cc * P:(cc + 1) * P] for cc in range(4 * n, 4 * n + 4)])
                if s >= 4:
                    cc = s - 4
                    tt = slice(cc * P, (cc + 1) * P)
                    if cc == 0:
                        pe.wait_ge(conv_done, i * 2 + 2)
                    pe.wait_ge(m_drained[0], m_count(0, i, F_CHUNK + cc))
                    if cc == 0:
                        pe.wait_ge(m_drained[1], m_count(1, i, F_CHUNK))
                        pe.wait_ge(state_zero, i + 1)
                    t.matmul(misc_ps[0][:, 0:P], m_k[:, tt], m_q[:, tt], start=True, stop=True)\
                        .then_inc(m_filled[0], 1)
                    pe.wait_ge(m_drained[2], m_count(2, i, cc))
                    t.matmul(misc_ps[2][:, 0:P + 1], m_ktok[:, cc], m_vtok[:, cc], start=True, stop=True)\
                        .then_inc(m_filled[2], 1)
                    pe.wait_ge(m_drained[1], m_count(1, i, F_CHUNK + cc))
                    t.matmul(misc_ps[1][:, 0:P + 1], m_q[:, tt], m_state[:], start=True, stop=True)\
                        .then_inc(qc_done, 1)

            def mlstm_second(i, s):
                if s >= 4:
                    cc = s - 4
                    pe.wait_ge(m_drained[0], m_count(0, i, F_CHUNK + cc) + 1)
                    t.matmul(misc_ps[1][:, 2 * P:3 * P + 1], m_s[:], m_vtok[:, cc], start=True, stop=True)\
                        .then_inc(m_filled[1], 1)

            def mlstm_third(i, s):
                if s == 2:
                    for n in range(2):
                        pe.wait_ge(m_drained[n], m_count(n, i, F_MK))
                        if n == 0:
                            pe.wait_ge(conv_done, i * 2 + 1)
                        transposes(n, [m_k[:, cc * P:(cc + 1) * P] for cc in range(4 * n, 4 * n + 4)])

            def iteration(i, last):
                segs, end = segments()
                project(i, 0, 24)
                for n in range(2):
                    pe.wait_ge(m_drained[n], m_count(n, i, F_V))
                    if n == 0:
                        pe.wait_ge(drained[1], job(i, -2) + 1)
                    transposes(n, [next_v[:, cc * P:(cc + 1) * P] for cc in range(4 * n, 4 * n + 4)])
                project(i, 24, PRE)
                pe.wait_ge(h_cols, i + 1)
                for n in range(2):
                    pe.wait_ge(m_drained[n], m_count(n, i, F_R))
                    t.matmul(misc_ps[n][:], sel_cur[0:32, :], bm[0:32, halves(n)], start=True, stop=True)\
                        .then_inc(m_filled[n], 1)
                for s in range(NS):
                    a, b, c_, d = segs[s]
                    scores(i, s)
                    if s > 0:
                        weighted_values(i, s - 1)
                    project(i, a, b)
                    mlstm_first(i, s)
                    project(i, b, c_)
                    mlstm_second(i, s)
                    exponents(i, s)
                    mlstm_third(i, s)
                    project(i, c_, d)
                project(i, segs[-1][3], end)
                weighted_values(i, NS - 1)
                if last:
                    project(0, 0, JOB_MM, base_job=J_GATES)
                for n in range(2):
                    pe.wait_ge(hn_done, i * NC + 4 * n + 4)
                    pe.wait_ge(m_drained[n], m_count(n, i, F_HN))
                    transposes(n, [m_num[:, cc, 0:P] for cc in range(4 * n, 4 * n + 4)])

            with pe.Fori(0, NH - 1) as i:
                iteration(i, False)
            iteration(NH - 1, True)

            for n in range(J_GATES + 1, J_MERGE):
                project(0, 0, JOB_MM, base_job=n)

            def merge_tile(m, u, first):
                for r in range(1 if first else 0, 3):
                    kt = NH if r else KT
                    for half in range(2):
                        pe.wait_ge(drained[half], merge_job(m, r))
                        for k in range(kt):
                            q = (0, 2, 3)[r] + k // 4
                            if half == 0 and k % 4 == 0:
                                pe.wait_ge(wL_done, merge_chunk(m, q) + 1)
                            if first and half == 0 and k == 0:
                                pe.wait_ge(yb_L, NH * r)
                            a = (ybH[r - 1], ybL[r - 1]) if r else (hH, hL)
                            slot = merge_slot(u, q)
                            ins = split_product(proj_ps[half][:], (wH[:, slot, k % 4], wL[:, slot, k % 4]),
                                                [z[:, k, halves(half)] for z in a], k, kt)
                            if r == 0 and half == 1 and k == 3:
                                ins.then_inc(w_first_used, 1)
                        ins.then_inc(filled[half], 1)

            merge_tile(0, 0, True)
            with pe.Fori(0, (KT - 2) // 3) as g:
                for u in range(3):
                    merge_tile(g * 3 + (u + 1), u + 1, False)
            merge_tile(KT - 1, KT - 1, False)

            pe.wait_ge(g_acc_step, KT)
            for n in range(2):
                pe.wait_ge(m_drained[n], m_count(n, NH, 0))
                t.matmul(misc_ps[n][:], ones[:], g_acc[:, halves(n)], start=True, stop=True)\
                    .then_inc(m_filled[n], 1)

            def out_product(q, half, k):
                return split_product((proj_ps, z_ps)[q][half][:], (yH[:, q, k], yL[:, q, k]),
                                     (hH[:, k, halves(half)], hL[:, k, halves(half)]), k, KT)

            for half in range(2):
                pe.wait_ge(drained[half], J_OUT)
            for k in range(KT):
                pe.wait_ge(woL_done, 2 * k + 2)
                for q in range(2):
                    if k == 0:
                        pe.wait_ge(yL_done, q + 1)
                    for half in range(2):
                        ins = out_product(q, half, k)
                        if k == KT - 1:
                            ins.then_inc(filled[half], 1)
            with pe.Fori(1, NC // 2) as r:
                for q in range(2):
                    pe.wait_ge(yL_done, r * 2 + q + 1)
                    for half in range(2):
                        pe.wait_ge(drained[half], r * 2 + (J_OUT + q - 1))
                        for k in range(KT):
                            ins = out_product(q, half, k)
                        ins.then_inc(filled[half], 1)

        @block.scalar
        def _(act):
            a = nc.scalar
            a.preload_act_table_set("natural_log_exp_and_others")

            for f in range(0, 2 * KT, 2):
                half, d = divmod(f, KT)
                act.wait_ge(m_filled[0], f // 2 + 2)
                a.activation(xT[:, d, halves(half)], misc_ps[0][:], ACT.Copy).then_inc(m_drained[0], 1)
                if f == 0:
                    act.wait_ge(cols_done, 1)
                    a.activation(small[:, 0:KT], cols[:, ROW_C:ROW_C + KT], ACT.Exp, scale=-1.0).then_inc(c_exp, 1)

            def split_high(slot, loads, freed, scale=1.0, width=P):
                act.wait_ge(w_in_s[slot], loads)
                if freed is not None:
                    act.wait_ge(*freed)
                a.activation(wH[:, slot, :, 0:width], w_raw[:, slot, :, 0:width], ACT.Copy, scale=scale)\
                    .then_inc(wH_done, 1)

            def pro_split(g):
                n = g // 2
                freed = None
                if g >= 3:
                    n3, odd = divmod(g - 3, 2)
                    freed = (filled[1] if odd else w_first_used, n3 + 1)
                split_high(g % 3, 16 * (g // 3 + 1), freed, SB_SCALE if n == 1 else 1.0, 2 * NH if n == 0 else P)

            for g in range(3):
                pro_split(g)
            for d in range(KT):
                act.wait_ge(h_full, d + 1)
                a.activation(hH[:, d], xT[:, d], ACT.Copy).then_inc(hH_done, 1)
                if d == 5:
                    pro_split(3)

            def bias_copy(dst, half, number, bias, rows=P):
                act.wait_ge(filled[half], number + 1)
                ps = (misc_ps if rows < P else proj_ps)[half]
                a.activation(dst, ps[0:rows, :], ACT.Identity, bias=bias, scale=1.0)\
                    .then_inc(drained[half], 1)

            def exp_into_sig(dst, half, number, bias, nbias, used=None):
                act.wait_ge(filled[half], number + 1)
                if used is not None:
                    act.wait_ge(sig_used, used)
                a.activation(sig[:, halves(half)], proj_ps[half][:], ACT.Exp, bias=nbias, scale=-1.0)\
                    .then_inc(sig_exp, 1)
                a.activation(dst[:, halves(half)], proj_ps[half][:], ACT.Identity, bias=bias, scale=1.0)\
                    .then_inc(drained[half], 1)

            for n in range(PRO_JOBS):
                for half in range(2):
                    if n == 0:
                        if half == 0:
                            act.wait_ge(bias_in, 16)
                            act.wait_ge(rows_zero, 5)
                        bias_copy(r_if[0:2 * NH, halves(half)], half, n, r_bias[0:2 * NH, :], 2 * NH)
                    elif n < 4:
                        b = cols[:, 4 * (n - 1):4 * (n - 1) + 1]
                        bias_copy((next_q, next_k, next_v)[n - 1][:, halves(half)], half, n, b)
                    else:
                        exp_into_sig(next_g, half, n, cols[:, 12:13], ncols[:, 12:13])
                    g = 2 * n + 3 + half
                    if 3 < g < 2 * PRO_JOBS + 2:
                        if g >= 2 * PRO_JOBS:
                            n3, odd = divmod(g - 3, 2)
                            split_high(g % 3, 16 * (g // 3 + 1), (filled[1] if odd else w_first_used, n3 + 1))
                        else:
                            pro_split(g)
                if n == 1:
                    act.wait_ge(rows_in, 16 * 8)
                    a.activation(r_e[:], r_f[:], ACT.Exp, scale=-1.0).then_inc(f_ln, 1)
                    act.wait_ge(f_ln, 1)
                    a.activation(r_e[:], r_e[:], ACT.Ln, bias=1.0).then_inc(f_ln, 1)
                if n == 3:
                    for q in range(1, 4):
                        r = slice(32 * q, 32 * q + 32)
                        act.wait_ge(q_rows, q)
                        a.activation(r_q[r, :], r_q[r, :], ACT.Exp).then_inc(q_exp, 1)

            def softplus_logs(i, s):
                f = first_col(s)
                for h in range(2):
                    act.wait_ge(z_done[h], i * NS + s + 1)
                    if s > 0:
                        act.wait_ge(pv_done[h], i * NS + s)
                    a.activation(soft[h][:, f:], z_ps[h][:, f:], ACT.Exp).then_inc(ex_done[h], 1)
                for h in range(2):
                    act.wait_ge(ex_done[h], i * NS + s + 1)
                    a.activation(soft[h][:, f:], soft[h][:, f:], ACT.Ln, bias=1.0).then_inc(ln_done[h], 1)

            def softplus_high(i, s):
                f = first_col(s)
                for h in range(2):
                    act.wait_ge(sp_done[h], i * NS + s + 1)
                    a.activation(spH[h][:, f:], soft[h][:, f:], ACT.Copy).then_inc(spH_done[h], 1)

            def attention_weights(i, s):
                f = first_col(s)
                for h in range(2):
                    act.wait_ge(e_done[h], i * NS + s + 1)
                    if not closes(s):
                        act.wait_ge(ts_sum[h], i * NCAR + carries(s) + 1)
                    a.activation(soft[h][:, f:], z_ps[h][:, f:], ACT.Exp).then_inc(a_exp[h], 1)

            def store_y(i, tc):
                act.wait_ge(y_staged, i * 2 + tc + 1)
                dst = ysb_dram[i] if isinstance(i, int) else ysb_dram[bass.ds(i, 1)].rearrange("a p s -> (a p) s")
                act.dma_start(dst[:, halves(tc)], y_stage[:]).then_inc(y_stored, 16)

            def gate_exp(dst, half, number, row):
                act.wait_ge(filled[half], number + 1)
                a.activation(dst[:, halves(half)], proj_ps[half][:], ACT.Exp, bias=ncols[:, row:row + 1],
                             scale=-1.0).then_inc(drained[half], 1)

            def gate_job(m):
                n = J_GATES + m - GATE_0
                for half in range(2):
                    gate_exp(yT[:, m], half, n, ROW_GSB + m)
                    g = 2 * n + 3 + half
                    split_high(g % 3, 16 * (g // 3 + 1), ((w_first_used, filled[1])[half], n + 1))

            def tasks(i, lo, hi, last):
                for what, n, half in events(lo, hi):
                    if what == "split":
                        cc = n
                        j3, odd = divmod(cc - 3, 2)
                        scale = SB_SCALE if (not last and cc // 2 < NJ and JOBS[cc // 2] == "sbq") else 1.0
                        slot = (2 * PRO_JOBS + cc) % 3
                        loads = i * (16 * 2 * NJ // 3) + 16 * ((2 * PRO_JOBS + cc) // 3 + 1)
                        split_high(slot, loads, (filled[1] if odd else w_first_used, job(i, j3) + 1), scale)
                        continue
                    if what == "o_log":
                        act.wait_ge(o_capped, i + 1)
                        a.activation(m_gate[:], m_gate[:], ACT.Ln, bias=1.0).then_inc(o_log, 1)
                        continue
                    if what == "z_log":
                        act.wait_ge(sig_capped, i * 2 + 2)
                        a.activation(sig[:], sig[:], ACT.Ln, bias=1.0).then_inc(sig_log, 1)
                        continue
                    if what == "z_exp":
                        act.wait_ge(z_sum, i + 1)
                        a.activation(sig[:], sig[:], ACT.Exp, scale=-1.0).then_inc(sig_done, 1)
                        continue
                    if what == "z_mul":
                        continue
                    name, number = (JOBS_LAST if last else JOBS)[n], job(i, n)
                    if name[0] == "g":
                        if half == 0:
                            act.wait_ge(pair_split, i * 4 + 4)
                            act.wait_ge(sig_used, i * 2 + 1)
                            act.wait_ge(m_filled[1], m_count(1, i, F_V) + 1)
                        gate_exp(sigm if name == "gml0" else yT[:, int(name[3])], half, number,
                                 ROW_GML if name == "gml0" else ROW_GSB + int(name[3]))
                    elif name == "mlv":
                        bias_copy(m_vraw[:, halves(half)], half, number, bias_of(name))
                    elif name in ("mlk", "mlq"):
                        if name == "mlk" and half == 0:
                            act.wait_ge(h_cols, i + 1)
                        if name == "mlq" and half == 0:
                            act.wait_ge(conv_acc, i * 4 + 2)
                        bias_copy(conv_in[:, 3 + half * HALF:3 + (half + 1) * HALF], half, number, bias_of(name))
                    elif name == "mlo":
                        act.wait_ge(filled[half], number + 1)
                        if half == 0:
                            act.wait_ge(m_drained[1], m_count(1, i, 0))
                        a.activation(m_gate[:, halves(half)], proj_ps[half][:], ACT.Exp,
                                     bias=bias_of(name, True), scale=-1.0).then_inc(drained[half], 1)
                    elif name == "mlz":
                        if half == 0:
                            act.wait_ge(conv_done, i * 2 + 2)
                        exp_into_sig(m_vraw, half, number, bias_of(name), bias_of(name, True), i * 2 + 1)
                    elif name == "sbz":
                        exp_into_sig(next_g, half, number, bias_of(name), bias_of(name, True), i * 2 + 2)
                    else:
                        if half == 0:
                            act.wait_ge(pair_split, i * 4 + 4)
                            if name == "sbv":
                                act.wait_ge(m_filled[1], m_count(1, i, F_V) + 1)
                        dst = {"sbq": next_q, "sbk": next_k, "sbv": next_v}[name]
                        bias_copy(dst[:, halves(half)], half, number, bias_of(name))

            by_chunk = lambda z: z.rearrange("p (c t) -> p c t", t=P)

            def conv_exps(i, k):
                act.wait_ge(conv_acc, i * 4 + 2 * k + 2)
                if k:
                    act.wait_ge(sig_used, i * 2 + 1)
                a.activation(conv_buffer(k), by_chunk((m_k, m_q)[k][:]), ACT.Exp, scale=-1.0).then_inc(conv_exp, 1)

            def conv_sigmoid(i, k):
                act.wait_ge(conv_cap, i * 2 + k + 1)
                e = conv_buffer(k)
                a.activation(e, e, ACT.Ln, bias=1.0).then_inc(conv_log, 1)
                act.wait_ge(conv_log, i * 2 + k + 1)
                a.activation(e, e, ACT.Exp, scale=-1.0).then_inc(conv_sig, 1)

            def token_major(i, bank_fill, dst):
                for n in range(2):
                    act.wait_ge(m_filled[n], m_count(n, i, bank_fill) + 1)
                    a.activation(dst[:, 4 * n:4 * n + 4, 0:P], misc_ps[n][:].rearrange("p (a b) -> p a b", a=4),
                                 ACT.Copy).then_inc(m_drained[n], 1)

            def place0(i, s):
                if s == 4:
                    store_y(i, 0)

            def place1(i, s):
                if s == 0:
                    act.wait_ge(w_sum, i + 1)
                    a.activation(m_w[:], m_w[:], ACT.Exp).then_inc(w_exp, 1)
                if s == 3:
                    token_major(i, F_MV, m_vtok)
                    conv_exps(i, 1)

            def place2(i, s):
                if s == 0:
                    conv_exps(i, 0)
                if s == 1:
                    conv_sigmoid(i, 0)
                if s == 3:
                    conv_sigmoid(i, 1)

            def iteration(i, last):
                segs, end = segments()
                act.wait_ge(sig_capped, i * 2 + 1)
                a.activation(sig[:], sig[:], ACT.Ln, bias=1.0).then_inc(sig_log, 1)
                tasks(i, -1, 24, last)
                token_major(i, F_V, v_tok)
                act.wait_ge(sig_log, i * 2 + 1)
                a.activation(sig[:], sig[:], ACT.Exp, scale=-1.0).then_inc(sig_done, 1)
                tasks(i, 24, PRE, last)
                for s in range(NS):
                    p0, p1, p2, p3 = segs[s]
                    softplus_logs(i, s)
                    tasks(i, p0, p1, last)
                    place0(i, s)
                    softplus_high(i, s)
                    tasks(i, p1, p2, last)
                    place1(i, s)
                    attention_weights(i, s)
                    place2(i, s)
                    tasks(i, p2, p3, last)
                act.wait_ge(var_done, i + 1)
                a.activation(small[:, 24:32], small[:, 16:24], ACT.Ln, bias=EPS).then_inc(rstd_ln, 1)
                act.wait_ge(rstd_ln, i + 1)
                a.activation(small[:, 24:32], small[:, 24:32], ACT.Exp, scale=-0.5).then_inc(rstd_exp, 1)
                tasks(i, segs[-1][3], end, last)
                store_y(i, 1)
                if last:
                    g = C_GATES + 2
                    split_high(g % 3, 16 * (g // 3 + 1), (filled[1], J_GATES))
                    act.wait_ge(sig_used, 2 * NH)
                    gate_job(GATE_0)
                for n in range(2):
                    act.wait_ge(m_drained[n], m_count(n, i, F_HN) + 1)
                dst = yml_dram[i] if isinstance(i, int) else yml_dram[bass.ds(i, 1)].rearrange("a p s -> (a p) s")
                act.dma_start(dst, m_w[:].rearrange("p a b -> p (a b)")).then_inc(yml_stored, 16)

            with act.Fori(0, NH - 1) as i:
                iteration(i, False)
            iteration(NH - 1, True)

            def gate_sigmoid(n):
                z = gate_buffer(n) if isinstance(n, int) else sigm
                act.wait_ge(g_capped, n + 1)
                a.activation(z[:], z[:], ACT.Ln, bias=1.0).then_inc(g_log, 1)
                act.wait_ge(g_log, n + 1)
                a.activation(z[:], z[:], ACT.Exp, scale=-1.0).then_inc(g_done, 1)

            def branch_high(n):
                act.wait_ge(y_in[n % 2], 16 * (n // 2 + 1))
                a.activation(ybH[n // NH][:, n % NH], stage[:, n % 2], ACT.Copy).then_inc(yb_H, 1)

            for n, m in enumerate(range(GATE_0 + 1, KT - 1)):
                gate_job(m)
                branch_high(2 * n)
                branch_high(2 * n + 1)
                gate_sigmoid(2 * n)
                gate_sigmoid(2 * n + 1)
            branch_high(2 * NH - 2)
            branch_high(2 * NH - 1)
            gate_job(KT - 1)

            def merge_tile(m, loads, u, first, last):
                def split(q, freed):
                    split_high(merge_slot(u, q), loads(q), freed)

                if not first:
                    for half in range(2):
                        act.wait_ge(drained[half], merge_job(m, 0))
                    for half in range(2):
                        act.wait_ge(filled[half], merge_job(m, 0) + 1)
                        if half:
                            split(3, (w_first_used, m + J_MERGE))
                        a.activation(sigm[:, halves(half)], proj_ps[half][:], ACT.Exp,
                                     bias=ncols[:, bass.ds(m + ROW_GML, 1)], scale=-1.0).then_inc(drained[half], 1)
                    if not last:
                        split(4, (filled[1], merge_job(m, 0) + 1))
                    gate_sigmoid(m + KT)
                if not last:
                    split(5, (filled[1], merge_job(m, 1) + 1))
                    split(6, (filled[1], merge_job(m, 2) + 1))

            def plain_loads(m):
                return lambda q: 16 * (merge_chunk(m, q) // 3 + 1)

            merge_tile(0, plain_loads(0), 0, True, False)
            for n in range(KT - 2, KT + 1):
                gate_sigmoid(n)
            with act.Fori(0, (KT - 2) // 3) as g:
                for u in range(1, 4):
                    merge_tile(g * 3 + u, lambda q: g * (16 * 4) + 16 * (merge_chunk(u, q) // 3 + 1), u, False, False)
            merge_tile(KT - 1, plain_loads(KT - 1), KT - 1, False, True)
            def w_out_high(lo, hi):
                for n in range(lo, hi):
                    act.wait_ge(wo_in[n % 7], 16 * (n // 7 + 1))
                    if n == 0:
                        act.wait_ge(filled[1], merge_job(KT - 1, 0) + 1)
                    a.activation(hH[:, n // 2, halves(n % 2)], wo_buffer[n % 7], ACT.Copy).then_inc(woH_done, 1)

            w_out_high(0, 8)

            def y_high(r, q, free):
                if free is not None:
                    act.wait_ge(filled[1], free)
                src = yT[:, :, bass.ds(r * 2 * P + q * P, P)]
                a.activation(yH[:, q], src, ACT.Copy).then_inc(yH_done, 1)

            def rstd(r, q):
                c0 = 8 * q
                act.wait_ge(var_done, r * 2 + (NH + q + 1))
                a.activation(small[:, c0 + 2:c0 + 3], small[:, c0 + 1:c0 + 2], ACT.Ln, bias=EPS).then_inc(rstd_ln, 1)
                act.wait_ge(rstd_ln, r * 2 + (NH + q + 1))
                a.activation(small[:, c0 + 2:c0 + 3], small[:, c0 + 2:c0 + 3], ACT.Exp, scale=-0.5)\
                    .then_inc(rstd_exp, 1)
                act.wait_ge(nbias_done, r * 2 + q + 1)
                a.activation(res[:, q], res[:, q], ACT.Identity, scale=small[:, c0 + 2:c0 + 3],
                             bias=small[:, c0 + 5:c0 + 6]).then_inc(normed, 1)

            act.wait_ge(yT_done, 2 * KT)
            act.wait_ge(filled[1], J_OUT)
            y_high(0, 0, None)
            y_high(0, 1, None)
            w_out_high(8, 2 * KT)

            def out_pair(r, last):
                for q in range(2):
                    if not last:
                        y_high(r + 1, q, r * 2 + (J_OUT + q + 1))
                    rstd(r, q)

            with act.Fori(0, NC // 2 - 1) as r:
                out_pair(r, False)
            out_pair(NC // 2 - 1, True)

        @block.vector
        def _(dve):
            v = nc.vector
            link = Chain(dve, dve_step)
            credit = 16

            dve.wait_ge(consts, 10)
            v.tensor_copy(neg_upto[:], upto[:]).then_inc(consts_r, 1)
            v.tensor_scalar(neg_ones[:], ones[:], -1.0, None, ALU.mult).then_inc(consts_r, 1)
            dve.wait_ge(m_filled[0], 1)
            link(v.tensor_copy(cols[:], misc_ps[0][:, 0:P]))
            link(v.tensor_scalar(cols[:, 0:4], cols[:, 0:4], SB_SCALE, None, ALU.mult))
            v.tensor_scalar(ncols[:], cols[:], -1.0, None, ALU.mult).then_inc(m_drained[0], 1)
            dve.wait_ge(m_drained[0], 1)
            dve.sem_inc(cols_done, 1)
            dve.wait_ge(c_exp, 1)
            link(v.tensor_scalar(small[:, 0:KT], small[:, 0:KT], 1.0, None, ALU.add))
            link(v.reciprocal(small[:, 8:16], small[:, 0:KT]))
            v.tensor_tensor(silu_c[:], cols[:, ROW_C:ROW_C + KT], small[:, 8:16], ALU.mult).then_inc(silu_done, 1)
            dve.wait_ge(silu_done, 1)

            def ada_rows(n):
                k, what = divmod(n, 2)
                dve.wait_ge(a_in[n % 4], 16 * (n // 4 + 1))
                acc = a_acc[:, what]
                if k == 0:
                    v.tensor_scalar(acc, a_raw[:, n % 4], silu_c[:, 0:1], None, ALU.mult).then_inc(ada_used, 1)
                else:
                    dve.wait_ge(ada_used, n - 1)
                    v.scalar_tensor_tensor(out=acc, in0=a_raw[:, n % 4], scalar=silu_c[:, k:k + 1], in1=acc,
                                           op0=ALU.mult, op1=ALU.add).then_inc(ada_used, 1)

            for n in range(2 * KT):
                if n < KT:
                    f = 2 * n + 1
                    half, d = divmod(f, KT)
                    dve.wait_ge(m_filled[1], f // 2 + 1)
                    v.tensor_copy(xT[:, d, halves(half)], misc_ps[1][:]).then_inc(m_drained[1], 1)
                ada_rows(n)

            def split_low(slot, number, scale=1.0, width=P):
                dve.wait_ge(wH_done, number)
                v.scalar_tensor_tensor(out=wL[:, slot, :, 0:width], in0=w_raw[:, slot, :, 0:width], scalar=scale,
                                       in1=wH[:, slot, :, 0:width], op0=ALU.mult, op1=ALU.subtract)\
                    .then_inc(wL_done, 1)

            def pro_split(g):
                n = g // 2
                split_low(g % 3, g + 1, SB_SCALE if n == 1 else 1.0, 2 * NH if n == 0 else P)

            for g in range(3):
                pro_split(g)

            def low_h(d):
                dve.wait_ge(hH_done, d + 1)
                v.tensor_tensor(hL[:, d], xT[:, d], hH[:, d], ALU.subtract).then_inc(hL_done, 1)

            def mod_columns(part, lo, hi):
                dve.wait_ge(ada_done, part + 1)
                z = z_ps[part]
                v.tensor_tensor(mod[:, 0, lo:hi], z[:, lo:hi], cols[:, ROW_ADA + lo:ROW_ADA + hi], ALU.add)\
                    .then_inc(mod_done, 1)
                v.scalar_tensor_tensor(out=mod[:, 1, lo:hi], in0=z[:, KT + lo:KT + hi], scalar=1.0,
                                       in1=cols[:, ROW_ADA + KT + lo:ROW_ADA + KT + hi], op0=ALU.add, op1=ALU.add)\
                    .then_inc(mod_done, 1)
                dve.wait_ge(mod_done, 2 * part + 2)

            dve.wait_ge(m_drained[0], 9)
            for d in range(KT):
                if d == 0:
                    mod_columns(0, 0, ADA_FIRST)
                if d == ADA_FIRST:
                    mod_columns(1, ADA_FIRST, KT)
                if d == 0:
                    dve.wait_ge(m_drained[1], 8)
                v.tensor_scalar(xT[:, d], xT[:, d], mod[:, 1, d:d + 1], mod[:, 0, d:d + 1], ALU.mult, ALU.add)\
                    .then_inc(h_full, 1)
                if d:
                    low_h(d - 1)
                if d == 6:
                    pro_split(3)
            low_h(KT - 1)

            def row_logs():
                dve.wait_ge(f_ln, 2)
                link(v.tensor_scalar(r_e[:], r_e[:], -1.0, -SOFT_CAP, ALU.mult, ALU.max))
                link(v.tensor_tensor(r_f[:], r_f[:], r_e[:], ALU.min))
                v.tensor_tensor_scan(r_b[:], r_one[:], r_f[:], 0.0, ALU.mult, ALU.add).then_inc(dve_step, 1)
                link.k += 1
                link(v.tensor_tensor_scan(r_m[:], r_f[:], r_i[:], 0.0, ALU.add, ALU.max))

            def row_columns():
                link.mark(v.tensor_tensor(bm[:], r_b[:], r_m[:], ALU.subtract))
                link(v.tensor_tensor(r_e[:], r_i[:], r_b[:], ALU.subtract))
                by = lambda z: z.rearrange("p (c t) -> p c t", t=P)
                v.tensor_copy(r_q[0:32, :], r_e[0:32, :]).then_inc(tok_done, 1)
                r = slice(32, 64)
                v.tensor_copy(r_q[r, 0:P], bm[r, 0:P]).then_inc(tok_done, 1)
                before = by(r_m[r, :])[:, 0:NC - 1, P - 1:P].to_broadcast((32, NC - 1, P))
                v.tensor_tensor(by(r_q[r, :])[:, 1:NC], by(bm[r, :])[:, 1:NC], before, ALU.add).then_inc(q_rows, 1)
                r = slice(64, 96)
                v.tensor_scalar(r_q[r, :], r_m[r, :], -1.0, None, ALU.mult).then_inc(q_rows, 1)
                r = slice(96, 128)
                ends = by(bm[r, :])[:, :, P - 1:P].to_broadcast((32, NC, P))
                v.tensor_tensor(by(r_q[r, :]), by(r_e[r, :]), ends, ALU.add).then_inc(q_rows, 1)

            for n in range(PRO_JOBS):
                for half in range(2):
                    g = 2 * n + 3 + half
                    if g == 3:
                        continue
                    if g < 2 * PRO_JOBS:
                        pro_split(g)
                    elif g < 2 * PRO_JOBS + 2:
                        split_low(g % 3, g + 1)
                if n == 2:
                    row_logs()
                if n == 3:
                    row_columns()
            for b in range(2):
                dve.wait_ge(m_filled[b], M_PRO[b])
                src = misc_ps[b][:].rearrange("p (c q r) -> p c q r", c=4, q=4)[:, :, :, 0:NH]
                v.tensor_copy(tok[:, 4 * b:4 * b + 4], src).then_inc(m_drained[b], 1)
            dve.wait_ge(m_filled[2], 1)
            v.tensor_copy(dec[:].rearrange("p c h -> p h c"),
                          misc_ps[2][:, 0:NH * NC].rearrange("p (h c) -> p h c", h=NH))\
                .then_inc(m_drained[2], 1)
            dve.wait_ge(m_drained[2], 1)
            v.memset(conv_in[:, 0:3], 0.0).then_inc(conv_pad, 1)
            v.memset(m_vtok[:, :, P:P + 1], 1.0).then_inc(conv_pad, 1)
            dve.sem_inc(y_stored, credit)
            dve.sem_inc(yml_stored, credit)
            link.base, link.k = link.base + link.k, 0

            def head_columns(i, last):
                dve.wait_ge(drained[1], job(i, 0))
                grp = cols[:, 0:36].rearrange("p (g h) -> p g h", h=NH)
                one = lambda lo: cols[:, bass.ds(i + lo, 1)]
                v.tensor_copy(h_col[:, 0:9], grp[:, :, bass.ds(i, 1)].rearrange("p g a -> p (g a)"))\
                    .then_inc(dve_step, 1)
                n = 1
                if not last:
                    v.tensor_copy(h_col[:, 9:18], grp[:, :, bass.ds(i + 1, 1)].rearrange("p g a -> p (g a)"))\
                        .then_inc(dve_step, 1)
                    n += 1
                taps = cols[:, ROW_CW:ROW_CW + 32].rearrange("p (j t) -> p j t", t=2 * NH)
                for which, lo in (("q", 0), ("k", NH)):
                    at_ = H_TAP[which]
                    v.tensor_copy(h_col[:, at_:at_ + 4], taps[:, :, bass.ds(i + lo, 1)].rearrange("p g a -> p (g a)"))\
                        .then_inc(dve_step, 1)
                    v.tensor_copy(h_col[:, H_CB[which]:H_CB[which] + 1], one(ROW_CB + lo)).then_inc(dve_step, 1)
                    n += 2
                v.tensor_copy(h_col[:, H_NG:H_NG + 1], one(ROW_NG)).then_inc(dve_step, 1)
                v.tensor_copy(h_tok[:], tok[:, :, :, bass.ds(i, 1)].rearrange("p c q a -> p q (c a)"))\
                    .then_inc(dve_step, 1)
                v.tensor_copy(h_dec[:], dec[:, :, bass.ds(i, 1)].rearrange("p c a -> p (c a)")).then_inc(dve_step, 1)
                n += 3
                link.k += n
                link(v.tensor_copy(sel_cur[:], sel_all[:, bass.ds(i, 1), :].rearrange("p a b -> p (a b)")))
                width = 9 if last else 18
                v.tensor_scalar(h_col[:, H_NEG:H_NEG + width], h_col[:, 0:width], -1.0, None, ALU.mult)\
                    .then_inc(h_cols, 1)
                v.memset(m_state[:], 0.0).then_inc(state_zero, 1)

            def split_pair(i):
                dve.wait_ge(drained[1], job(i, -3) + 1)
                for n, (src, hi, lo) in enumerate(((next_k, kH, kL), (next_q, qH, qL))):
                    v.tensor_copy(hi[:], src[:]).then_inc(pair_split, 1)
                    dve.wait_ge(pair_split, i * 4 + (2 * n + 1))
                    v.tensor_tensor(lo[:], src[:], hi[:], ALU.subtract).then_inc(pair_split, 1)

            def sum_zero(i, s):
                if opens(s):
                    for h in range(2):
                        if s > 0:
                            dve.wait_ge(tsL_done[h], i * NCAR + carries(s))
                        v.memset(tsum[h][:], 0.0).then_inc(ts_zero[h], 1)

            def softplus(i, s):
                f = first_col(s)
                for h in range(2):
                    dve.wait_ge(ln_done[h], i * NS + s + 1)
                    v.scalar_tensor_tensor(out=soft[h][:, f:], in0=soft[h][:, f:], scalar=SOFT_CAP, in1=z_ps[h][:, f:],
                                           op0=ALU.min, op1=ALU.max)\
                        .then_inc(sp_raw[h] if diagonal(s) else sp_done[h], 1)
                if diagonal(s):
                    for h in range(2):
                        dve.wait_ge(sp_raw[h], i * ND + diagonals(s) + 1)
                        d = soft[h][:, f:f + P]
                        v.tensor_tensor(d, d, later[:], ALU.mult).then_inc(sp_done[h], 1)

            def softplus_low(i, s):
                f = first_col(s)
                for h in range(2):
                    dve.wait_ge(spH_done[h], i * NS + s + 1)
                    v.tensor_tensor(spL[h][:, f:], soft[h][:, f:], spH[h][:, f:], ALU.subtract)\
                        .then_inc(spL_done[h], 1)

            def carry_high(i, s):
                if closes(s):
                    return
                f = first_col(s)
                for h in range(2):
                    dve.wait_ge(ts_sum[h], i * NCAR + carries(s) + 1)
                    dve.wait_ge(e_done[h], i * NS + s + 1)
                    v.tensor_copy(tsH[h][:, f:], tsum[h][:, f:]).then_inc(tsH_done[h], 1)

            def mask_weights(i, s):
                if not diagonal(s):
                    return
                f = first_col(s)
                for h in range(2):
                    dve.wait_ge(a_exp[h], i * NS + s + 1)
                    d = soft[h][:, f:f + P]
                    v.scalar_tensor_tensor(out=d, in0=d, scalar=3.0e38, in1=later[:], op0=ALU.min, op1=ALU.mult)\
                        .then_inc(a_mask[h], 1)

            def gate_y(i, tc):
                for h in range(2):
                    dve.wait_ge(pv_done[h], i * NS + (4 if tc == 0 else NS))
                dve.wait_ge(y_stored, i * 32 + (credit + 16 * tc))
                v.tensor_tensor(y_stage[:], y_ps[:], g_cur[:, halves(tc)], ALU.mult).then_inc(y_staged, 1)

            def tasks(i, lo, hi, last):
                for what, n, half in events(lo, hi):
                    if what == "split":
                        scale = SB_SCALE if (not last and n // 2 < NJ and JOBS[n // 2] == "sbq") else 1.0
                        split_low((2 * PRO_JOBS + n) % 3, chunk(i, n) + 1, scale)
                        continue
                    if what == "o_log":
                        for h in range(2):
                            dve.wait_ge(drained[h], job(i, 3) + 1)
                        v.tensor_scalar(m_gate[:], m_gate[:], EXP_CAP, None, ALU.min).then_inc(o_capped, 1)
                    elif what == "z_log":
                        cap_sig(i * 2 + 1)
                    elif what == "z_exp":
                        dve.wait_ge(sig_log, i * 2 + 2)
                        dve.wait_ge(o_log, i + 1)
                        v.tensor_tensor(sig[:], sig[:], m_gate[:], ALU.add).then_inc(z_sum, 1)
                    elif what == "z_mul":
                        dve.wait_ge(drained[1], job(i, 4) + 1)
                        dve.wait_ge(sig_done, i * 2 + 2)
                        v.tensor_tensor(m_gate[:], sig[:], m_vraw[:], ALU.mult).then_inc(sig_used, 1)
                        dve.wait_ge(sig_used, i * 2 + 2)
                        dve.sem_inc(m_gate_done, 1)

            def cap_sig(use):
                dve.wait_ge(sig_exp, use * 2 + 2)
                v.tensor_scalar(sig[:], sig[:], EXP_CAP, None, ALU.min).then_inc(sig_capped, 1)

            def pair_gate(i):
                dve.wait_ge(sig_done, i * 2 + 1)
                v.tensor_tensor(g_cur[:], next_g[:], sig[:], ALU.mult).then_inc(sig_used, 1)
                dve.wait_ge(sig_used, i * 2 + 1)

            def conv_sum(i, k):
                which, half = ("k", "q")[k // 2], k % 2
                dst = (m_k, m_q)[k // 2][:, halves(half)]
                tap = lambda j: h_col[:, H_TAP[which] + j:H_TAP[which] + j + 1]
                src = lambda j: conv_in[:, half * HALF + j:half * HALF + j + HALF]
                dve.wait_ge(drained[half], job(i, k // 2) + 1)
                link(v.tensor_scalar(dst, src(3), tap(3), h_col[:, H_CB[which]:H_CB[which] + 1], ALU.mult, ALU.add))
                for j in (2, 1):
                    link(v.scalar_tensor_tensor(out=dst, in0=src(j), scalar=tap(j), in1=dst, op0=ALU.mult,
                                                op1=ALU.add))
                v.scalar_tensor_tensor(out=dst, in0=src(0), scalar=tap(0), in1=dst, op0=ALU.mult, op1=ALU.add)\
                    .then_inc(conv_acc, 1)

            def conv_bound(i, k):
                dve.wait_ge(conv_exp, i * 2 + k + 1)
                v.tensor_scalar(conv_buffer(k), conv_buffer(k), EXP_CAP, None, ALU.min).then_inc(conv_cap, 1)

            def conv_silu(i, k):
                dst = (m_k, m_q)[k][:].rearrange("p (c t) -> p c t", t=P)
                dve.wait_ge(conv_sig, i * 2 + k + 1)
                v.scalar_tensor_tensor(out=dst, in0=conv_buffer(k), scalar=ML_SCALE if k else 1.0, in1=dst,
                                       op0=ALU.mult, op1=ALU.mult).then_inc(conv_done, 1)

            def chunk_weights(i):
                dve.wait_ge(yml_stored, i * 16 + credit)
                for n in range(2):
                    dve.wait_ge(m_filled[n], m_count(n, i, F_R) + 1)
                    u = h_tok[:, 0, 4 * n:4 * n + 4].unsqueeze(2).to_broadcast((P, 4, P))
                    v.tensor_tensor(m_w[:, 4 * n:4 * n + 4], misc_ps[n][:].rearrange("p (a b) -> p a b", a=4), u,
                                    ALU.add).then_inc(m_drained[n], 1)
                    dve.wait_ge(m_drained[n], m_count(n, i, F_R) + 1)
                v.tensor_scalar(m_w[:], m_w[:], 0.0, None, ALU.min).then_inc(w_sum, 1)

            def mask_chunk_weights(i):
                dve.wait_ge(w_exp, i + 1)
                v.tensor_tensor(m_w[:], m_w[:], notbefore[:].unsqueeze(1).to_broadcast((P, NC, P)), ALU.mult)\
                    .then_inc(w_mask, 1)

            def weighted_keys(i):
                for n in range(2):
                    dve.wait_ge(m_filled[n], m_count(n, i, F_MK) + 1)
                    w = h_tok[:, 3, 4 * n:4 * n + 4].unsqueeze(2).to_broadcast((P, 4, P))
                    v.tensor_tensor(m_ktok[:, 4 * n:4 * n + 4], misc_ps[n][:].rearrange("p (a b) -> p a b", a=4), w,
                                    ALU.mult).then_inc(m_drained[n], 1)

            def chunk_scores(i, cc):
                dve.wait_ge(m_filled[0], m_count(0, i, F_CHUNK + cc) + 1)
                if cc == 0:
                    dve.wait_ge(w_mask, i + 1)
                v.tensor_tensor(m_s[:], misc_ps[0][:, 0:P], m_w[:, cc], ALU.mult).then_inc(m_drained[0], 1)
                dve.wait_ge(m_filled[2], m_count(2, i, cc) + 1)
                dve.wait_ge(qc_done, i * NC + cc + 1)
                v.scalar_tensor_tensor(out=m_state[:], in0=m_state[:], scalar=h_dec[:, cc:cc + 1],
                                       in1=misc_ps[2][:, 0:P + 1], op0=ALU.mult, op1=ALU.add)\
                    .then_inc(m_drained[2], 1)

            def aggregate(cc):
                link.mark(v.bn_aggr(mv[:, cc], stat[:, cc]))

            def chunk_values(i, cc):
                dve.wait_ge(m_filled[1], m_count(1, i, F_CHUNK + cc) + 1)
                link(v.tensor_scalar(m_tmp[:], misc_ps[1][:, 0:P + 1], h_tok[:, 1, cc:cc + 1], None, ALU.mult))
                v.tensor_tensor(m_num[:, cc], misc_ps[1][:, 2 * P:3 * P + 1], m_tmp[:], ALU.add)\
                    .then_inc(m_drained[1], 1)
                if cc:
                    aggregate(cc - 1)
                dve.wait_ge(m_drained[1], m_count(1, i, F_CHUNK + cc) + 1)
                link.mark(v.bn_stats(stat[:, cc], m_num[:, cc, 0:P]))

            def newton(y, var, tmp):
                link(v.tensor_tensor(tmp, y, y, ALU.mult))
                link(v.scalar_tensor_tensor(out=tmp, in0=var, scalar=EPS, in1=tmp, op0=ALU.add, op1=ALU.mult))
                link(v.tensor_scalar(tmp, tmp, -0.5, 1.5, ALU.mult, ALU.add))
                link(v.tensor_tensor(y, y, tmp, ALU.mult))

            def norm_head(i):
                den, rden, var, y, tmp, rr = [small[:, 8 * n:8 * n + 8] for n in range(6)]
                link(v.tensor_copy(den, m_num[:, :, P]))
                link.mark(v.scalar_tensor_tensor(out=rden, in0=den, scalar=-1.0, in1=den, op0=ALU.mult, op1=ALU.max))
                aggregate(NC - 1)
                link.wait()
                link(v.tensor_tensor(den, rden, h_tok[:, 2, :], ALU.max))
                link(v.reciprocal(rden, den))
                link(v.tensor_tensor(tmp, rden, rden, ALU.mult))
                v.tensor_tensor(var, mv[:, :, 1], tmp, ALU.mult).then_inc(var_done, 1)
                dve.wait_ge(rstd_exp, i + 1)
                newton(y, var, tmp)
                link(v.tensor_tensor(rr, y, rden, ALU.mult))
                for cc in range(NC):
                    v.tensor_scalar(m_num[:, cc, 0:P], m_num[:, cc, 0:P], mv[:, cc, 0:1], rr[:, cc:cc + 1],
                                    ALU.subtract, ALU.mult).then_inc(hn_done, 1)

            def gate_head(i):
                for n in range(2):
                    dve.wait_ge(m_gate_done, i + 1)
                    dve.wait_ge(m_filled[n], m_count(n, i, F_HN) + 1)
                    v.scalar_tensor_tensor(out=m_w[:, 4 * n:4 * n + 4].rearrange("p a b -> p (a b)"),
                                           in0=misc_ps[n][:], scalar=h_col[:, H_NG:H_NG + 1],
                                           in1=m_gate[:, halves(n)], op0=ALU.mult, op1=ALU.mult)\
                        .then_inc(m_drained[n], 1)
                for n in range(2):
                    dve.wait_ge(m_drained[n], m_count(n, i, F_HN) + 1)

            def place0(i, s):
                if s == 4:
                    gate_y(i, 0)
                if s >= 4:
                    chunk_scores(i, s - 4)

            def place1(i, s):
                if s == 0:
                    conv_sum(i, 1)
                if s == 1:
                    conv_bound(i, 0)
                if s >= 4:
                    chunk_values(i, s - 4)

            def place2(i, s):
                if s == 0:
                    mask_chunk_weights(i)
                    pair_gate(i)
                if s == 1:
                    conv_sum(i, 2)
                if s == 2:
                    weighted_keys(i)
                    conv_sum(i, 3)
                if s == 3:
                    conv_bound(i, 1)
                    conv_silu(i, 1)

            def iteration(i, last):
                segs, end = segments()
                split_pair(i)
                cap_sig(i * 2)
                head_columns(i, last)
                tasks(i, -1, 24, last)
                conv_sum(i, 0)
                tasks(i, 24, PRE, last)
                chunk_weights(i)
                for s in range(NS):
                    p0, p1, p2, p3 = segs[s]
                    sum_zero(i, s)
                    if s == 2:
                        conv_silu(i, 0)
                    softplus(i, s)
                    place0(i, s)
                    tasks(i, p0, p1, last)
                    softplus_low(i, s)
                    tasks(i, p1, p2, last)
                    place1(i, s)
                    mask_weights(i, s)
                    carry_high(i, s)
                    place2(i, s)
                    tasks(i, p2, p3, last)
                norm_head(i)
                tasks(i, segs[-1][3], end, last)
                gate_y(i, 1)
                if last:
                    for g in range(C_GATES + 2, C_GATES + 5):
                        split_low(g % 3, g + 1)
                gate_head(i)

            per = 56
            with dve.Fori(0, NH - 1) as i:
                link.enter(i, per)
                iteration(i, False)
            link.leave(NH - 1, "iteration")
            link.enter(0, 0)
            iteration(NH - 1, True)
            link.base, link.k = link.base + link.k, 0

            dve.sem_inc(free, 1)

            def cap_gate(n, job_number):
                z = gate_buffer(n) if isinstance(n, int) else sigm
                for half in range(2):
                    dve.wait_ge(drained[half], job_number + 1)
                v.tensor_scalar(z[:], z[:], EXP_CAP, None, ALU.min).then_inc(g_capped, 1)

            def gate_sum(k):
                dve.wait_ge(raw_in[k % 2], 16 * (k // 2 + 1))
                if k == 0:
                    v.tensor_scalar(g_acc[:], raw[:, 0], silu_c[:, 0:1], None, ALU.mult).then_inc(g_acc_step, 1)
                else:
                    v.scalar_tensor_tensor(out=g_acc[:], in0=raw[:, k % 2], scalar=silu_c[:, k:k + 1], in1=g_acc[:],
                                           op0=ALU.mult, op1=ALU.add).then_inc(g_acc_step, 1)
                dve.wait_ge(g_acc_step, k + 1)

            def branch_low(n):
                dve.wait_ge(yb_H, n + 1)
                v.tensor_tensor(ybL[n // NH][:, n % NH], stage[:, n % 2], ybH[n // NH][:, n % NH], ALU.subtract)\
                    .then_inc(yb_L, 1)

            def freed_low(m):
                for half in range(2):
                    g = 2 * (J_GATES + m - GATE_0) + 3 + half
                    split_low(g % 3, g + 1)

            for n, m in enumerate(range(GATE_0 + 1, KT - 1)):
                freed_low(m)
                cap_gate(2 * n, J_GATES - 4 + 2 * n)
                cap_gate(2 * n + 1, J_GATES - 3 + 2 * n)
                branch_low(2 * n)
                branch_low(2 * n + 1)
                gate_sum(2 * n)
                gate_sum(2 * n + 1)
            branch_low(2 * NH - 2)
            branch_low(2 * NH - 1)
            freed_low(KT - 1)

            def merge_tile(m, u, first, last):
                def split(q):
                    split_low(merge_slot(u, q), merge_chunk(m, q) + 1)

                if not first:
                    split(3)
                    if not last:
                        split(4)
                    cap_gate(m + KT, merge_job(m, 0))
                if last:
                    w_out_low(0, 2)
                row = lambda half: yT[:, bass.ds(m, 1), halves(half)].rearrange("p a s -> p (a s)")
                for half in range(2):
                    dve.wait_ge(filled[half], merge_job(m, 1) + 1)
                    if half == 0:
                        dve.wait_ge(g_done, m + 2)
                    v.tensor_tensor(row(half), proj_ps[half][:], row(half), ALU.mult).then_inc(drained[half], 1)
                if last:
                    w_out_low(2, 5)
                else:
                    split(5)
                for half in range(2):
                    dve.wait_ge(filled[half], merge_job(m, 2) + 1)
                    if half == 0:
                        dve.wait_ge(g_done, 1 if first else m + (KT + 1))
                    v.tensor_tensor(m_prod[:], proj_ps[half][:], sigm[:, halves(half)], ALU.mult)\
                        .then_inc(drained[half], 1)
                    dve.wait_ge(drained[half], merge_job(m, 2) + 1)
                    v.tensor_tensor(row(half), row(half), m_prod[:], ALU.add).then_inc(yT_done, 1)
                    dve.wait_ge(yT_done, m * 2 + (half + 1))
                if not last:
                    split(6)

            def w_out_low(lo, hi):
                for n in range(lo, hi):
                    dve.wait_ge(woH_done, n + 1)
                    v.tensor_tensor(hL[:, n // 2, halves(n % 2)], wo_buffer[n % 7],
                                    hH[:, n // 2, halves(n % 2)], ALU.subtract).then_inc(woL_done, 1)

            merge_tile(0, 0, True, False)
            for n in range(KT - 2, KT + 1):
                cap_gate(n, J_GATES - 4 + n)
            gate_sum(KT - 2)
            gate_sum(KT - 1)
            with dve.Fori(0, (KT - 2) // 3) as g:
                for u in range(1, 4):
                    merge_tile(g * 3 + u, u, False, False)
            merge_tile(KT - 1, KT - 1, False, True)

            for q in range(2):
                dve.wait_ge(yH_done, q + 1)
                v.tensor_tensor(yL[:, q], yT[:, :, q * P:(q + 1) * P], yH[:, q], ALU.subtract).then_inc(yL_done, 1)
            w_out_low(5, 2 * KT)
            dve.wait_ge(bc_in, 48)
            for n in range(2):
                dve.wait_ge(m_filled[n], m_count(n, NH, 0) + 1)
                h = halves(n)
                v.scalar_tensor_tensor(out=gate1[:, h], in0=misc_ps[n][:], scalar=1.0, in1=gate1[:, h],
                                       op0=ALU.add, op1=ALU.add).then_inc(gate_done, 1)

            dve.wait_ge(gate_done, 2)

            def finish_tile(r, q):
                row = res[:, q]
                dve.wait_ge(normed, r * 2 + q + 1)
                link(v.tensor_tensor(row, row, lng[:], ALU.mult))
                v.tensor_tensor(row, row, lnb[:], ALU.add).then_inc(out_done, 1)

            def norm_tile(r, q, first, last):
                row = res[:, q]
                if not first:
                    dve.wait_ge(stored[q], r * 16)
                for part in ((0,), (1,)) if q and last else ((0, 1),):
                    for half in part:
                        h = halves(half)
                        dve.wait_ge(filled[half], r * 2 + (J_OUT + q + 1))
                        v.tensor_tensor(row[:, h], (proj_ps, z_ps)[q][half][:], gate1[:, h], ALU.mult)\
                            .then_inc(drained[half], 1)
                    for half in part:
                        dve.wait_ge(drained[half], r * 2 + (J_OUT + q + 1))
                    dve.wait_ge(x_tile_in[q], r * 16 + 16)
                    h = slice(part[0] * HALF, (part[-1] + 1) * HALF)
                    link(v.scalar_tensor_tensor(out=row[:, h], in0=x_in[:, q, h], scalar=ALPHA, in1=row[:, h],
                                                op0=ALU.mult, op1=ALU.add))
                    for half in part:
                        link.mark(v.bn_stats(stat_out[:, q, half], row[:, halves(half)]))
                link.wait()
                if q and not last:
                    finish_tile(r, 0)
                elif not q and not first:
                    finish_tile(r - 1, 1)
                c0 = 8 * q
                v.bn_aggr(small[:, c0:c0 + 2], stat_out[:, q].rearrange("p a b -> p (a b)")).then_inc(var_done, 1)
                dve.wait_ge(rstd_exp, r * 2 + (NH + q + 1))
                newton(small[:, c0 + 2:c0 + 3], small[:, c0 + 1:c0 + 2], small[:, c0 + 3:c0 + 4])
                v.scalar_tensor_tensor(out=small[:, c0 + 5:c0 + 6], in0=small[:, c0:c0 + 1], scalar=-1.0,
                                       in1=small[:, c0 + 2:c0 + 3], op0=ALU.mult, op1=ALU.mult).then_inc(nbias_done, 1)
                if q and last:
                    finish_tile(r, 0)

            def out_pair(r, first, last):
                for q in range(2):
                    norm_tile(r, q, first, last)

            out_pair(0, True, False)
            link.base, link.k = link.base + link.k, 0
            with dve.Fori(1, NC // 2 - 1) as r:
                link.enter(r - 1, 16)
                out_pair(r, False, False)
            link.leave(NC // 2 - 2, "output")
            out_pair(NC // 2 - 1, False, True)
            finish_tile(NC // 2 - 1, 1)


_INS = ["x", "c", "w_ada", "b_ada", "w_in", "b_in", "conv_w", "conv_b", "ml_norm_g", "w_sb_proj", "w_ml_proj",
        "w_out", "ln_g", "ln_b"]


def kernel(**inputs):
    import numpy as _np
    import concourse.bacc as _bacc
    from concourse.bass_utils import run_bass_kernel_spmd as _run

    nc = _bacc.Bacc("TRN2", target_bir_lowering=False, num_devices=1)
    arrays, args = {}, []
    for name in _INS:
        a = _np.ascontiguousarray(inputs[name])
        arrays[f"in_{name}"] = a
        args.append(nc.dram_tensor(f"in_{name}", a.shape, mybir.dt.from_np(a.dtype), kind="ExternalInput").ap())
    out = nc.dram_tensor("out_y", (1, S, D), F32, kind="ExternalOutput").ap()
    build_kernel(nc, *args, out)
    r = _run(nc, [arrays], core_ids=[0])
    return r.results[0]["out_y"]
```
